# Optimizing a Trainium2 kernel written in Bass

```python
import jax, jax.numpy as jnp
from jax import lax
import numpy as np

D_MODEL = 1024
BATCH = 1
SEQ = 128
DEPTH = 4
DEC_BATCH = 1
DEC_SEQ = 256
PAST_LEN = 128

GRID_W = 64
N_MIXERS = 3
N_POOL_LAYERS = (DEPTH + 2) // 3
N_MLSTM_LAYERS = (DEPTH + 1) // 3
N_MLA_LAYERS = DEPTH // 3
NORM_EPS = 1e-6

POOL_WINDOWS = (2, 4, 8, 16)
POOL_GROUPS = 4
POOL_GW = D_MODEL // POOL_GROUPS

MLSTM_HEADS = 4
MLSTM_DV = D_MODEL // MLSTM_HEADS
MLSTM_DK = MLSTM_DV // 2
MLSTM_CHUNK = 64
MLSTM_IN = 2 * MLSTM_HEADS * MLSTM_DK + 2 * MLSTM_HEADS * MLSTM_DV + 4 * MLSTM_HEADS

MLA_HEADS = 8
MLA_NOPE = 128
MLA_ROPE = 64
MLA_V = 128
MLA_Q_LORA = 512
MLA_KV_LORA = 256
MLA_IN = MLA_Q_LORA + MLA_KV_LORA + MLA_ROPE
ATTN_SCALE = (MLA_NOPE + MLA_ROPE) ** -0.5
ROPE_BASE = 10000.0
Q_BLOCK = 128

N_EXPERTS = 16
N_EXPERT_GROUPS = 4
EXPERTS_PER_GROUP = N_EXPERTS // N_EXPERT_GROUPS
TOP_K = 2
D_EXPERT = 256

kernel_name = "hybrid_pool_mlstm_mla_moe_diffusion_step"

def rmsnorm(x, g):
    xf = x.astype(jnp.float32)
    y = xf * lax.rsqrt(jnp.mean(xf * xf, axis=-1, keepdims=True) + NORM_EPS)
    return (y * g.astype(jnp.float32)).astype(x.dtype)

def ada_mod(cvec, w, b):
    m = jax.nn.silu(cvec) @ w + b
    return m.reshape(cvec.shape[0], 6, D_MODEL)

def modulate(h, shift, scale):
    return h * (1.0 + scale[:, None, :]) + shift[:, None, :]

def pool_mixer(h, w_pool, scale):
    B, N, D = h.shape
    hf = h.astype(jnp.float32)
    cs = jnp.pad(jnp.cumsum(hf, axis=1), ((0, 0), (1, 0), (0, 0)))
    t = jnp.arange(N)
    outs = []
    for g, w in enumerate(POOL_WINDOWS):
        lo = jnp.clip(t - w // 2, 0, N)
        hi = jnp.clip(t + w // 2, 0, N)
        cg = cs[:, :, g * POOL_GW:(g + 1) * POOL_GW]
        mean = (cg[:, hi] - cg[:, lo]) / (hi - lo).astype(jnp.float32)[None, :, None]
        outs.append(mean - hf[..., g * POOL_GW:(g + 1) * POOL_GW])
    pooled = jnp.stack(outs, axis=2).astype(h.dtype)
    y = jnp.einsum("bngc,gcd->bngd", pooled, w_pool).reshape(B, N, D)
    return y * scale

def mlstm_zero_state(b):
    return (jnp.zeros((b, MLSTM_HEADS, MLSTM_DK, MLSTM_DV), jnp.float32),
            jnp.zeros((b, MLSTM_HEADS, MLSTM_DK), jnp.float32),
            jnp.zeros((b, MLSTM_HEADS), jnp.float32))

def mlstm_chunkwise(q, k, v, i_raw, f_raw, state):
    C0, n0, m0 = (s.astype(jnp.float32) for s in state)
    B, H, N, _ = q.shape
    L = MLSTM_CHUNK
    nc = N // L

    def chunks(a):
        return jnp.moveaxis(a.reshape(a.shape[:2] + (nc, L) + a.shape[3:]), 2, 0)

    inputs = (chunks(q.astype(jnp.float32)), chunks(k.astype(jnp.float32)),
              chunks(v.astype(jnp.float32)), chunks(i_raw.astype(jnp.float32)),
              chunks(jax.nn.log_sigmoid(f_raw.astype(jnp.float32))))
    tri = jnp.tril(jnp.ones((L, L), dtype=bool))

    def step(carry, inp):
        C, n, m = carry
        qc, kc, vc, ic, lfc = inp
        b = jnp.cumsum(lfc, axis=-1)
        logD = jnp.where(tri, b[..., :, None] - b[..., None, :] + ic[..., None, :], -jnp.inf)
        log_state = b + m[..., None]
        m_t = jnp.maximum(log_state, jnp.max(logD, axis=-1))
        Dw = jnp.exp(logD - m_t[..., None])
        sw = jnp.exp(log_state - m_t)
        A = jnp.einsum("bhtd,bhsd->bhts", qc, kc) * Dw
        num = sw[..., None] * jnp.einsum("bhtd,bhde->bhte", qc, C) + jnp.einsum("bhts,bhse->bhte", A, vc)
        den = sw * jnp.einsum("bhtd,bhd->bht", qc, n) + jnp.sum(A, axis=-1)
        h = num / jnp.maximum(jnp.abs(den), jnp.exp(-m_t))[..., None]
        bL = b[..., -1]
        log_k = bL[..., None] - b + ic
        m_new = jnp.maximum(bL + m, jnp.max(log_k, axis=-1))
        kw = jnp.exp(log_k - m_new[..., None])
        decay = jnp.exp(bL + m - m_new)
        C_new = decay[..., None, None] * C + jnp.einsum("bhs,bhsd,bhse->bhde", kw, kc, vc)
        n_new = decay[..., None] * n + jnp.einsum("bhs,bhsd->bhd", kw, kc)
        return (C_new, n_new, m_new), h

    (C, n, m), hs = lax.scan(step, (C0, n0, m0), inputs)
    h = jnp.moveaxis(hs, 0, 2).reshape(B, H, N, MLSTM_DV)
    return h, (C, n, m)

def mlstm_mixer(h, w_in, b_gate, head_g, w_out, init_f, init_b):
    B, N, _ = h.shape
    hk, hv = MLSTM_HEADS * MLSTM_DK, MLSTM_HEADS * MLSTM_DV
    proj = h @ w_in

    def heads(a, d):
        return a.reshape(B, N, MLSTM_HEADS, d).transpose(0, 2, 1, 3)

    q = heads(proj[..., :hk], MLSTM_DK) * (MLSTM_DK ** -0.5)
    k = heads(proj[..., hk:2 * hk], MLSTM_DK)
    v = heads(proj[..., 2 * hk:2 * hk + hv], MLSTM_DV)
    o = proj[..., 2 * hk + hv:2 * hk + 2 * hv]
    g = (proj[..., 2 * hk + 2 * hv:].reshape(B, N, 4, MLSTM_HEADS) + b_gate).transpose(2, 0, 3, 1)
    h_f, st_f = mlstm_chunkwise(q, k, v, g[0], g[1], init_f)
    fl = lambda a: jnp.flip(a, axis=2)
    h_b, st_b = mlstm_chunkwise(fl(q), fl(k), fl(v), fl(g[2]), fl(g[3]), init_b)
    hs = h_f + fl(h_b)
    hs = hs * lax.rsqrt(jnp.mean(hs * hs, axis=-1, keepdims=True) + NORM_EPS)
    hs = hs.transpose(0, 2, 1, 3).reshape(B, N, hv) * head_g.astype(jnp.float32)
    y = (jax.nn.sigmoid(o.astype(jnp.float32)) * hs).astype(h.dtype) @ w_out
    return y, st_f, st_b

def rope_1d(x, pos):
    d = x.shape[-1]
    half = d // 2
    freq = jnp.power(ROPE_BASE, -jnp.arange(half, dtype=jnp.float32) / half)
    ang = pos.astype(jnp.float32)[:, None] * freq[None, :]
    shape = (x.shape[1],) + (1,) * (x.ndim - 3) + (d,)
    cos = jnp.concatenate([jnp.cos(ang), jnp.cos(ang)], -1).reshape(shape).astype(x.dtype)
    sin = jnp.concatenate([jnp.sin(ang), jnp.sin(ang)], -1).reshape(shape).astype(x.dtype)
    rot = jnp.concatenate([-x[..., half:], x[..., :half]], -1)
    return x * cos + rot * sin

def rope_axial(x, n):
    rows = n // GRID_W
    row = jnp.repeat(jnp.arange(rows), GRID_W)
    col = jnp.tile(jnp.arange(GRID_W), rows)
    r = MLA_ROPE // 2
    return jnp.concatenate([rope_1d(x[..., :r], row), rope_1d(x[..., r:], col)], -1)

def mla_project(h, w_in, q_g, kv_g, w_qb):
    B, N, _ = h.shape
    proj = h @ w_in
    q_lat = proj[..., :MLA_Q_LORA]
    ckv = rmsnorm(proj[..., MLA_Q_LORA:MLA_Q_LORA + MLA_KV_LORA], kv_g)
    kpe = proj[..., MLA_Q_LORA + MLA_KV_LORA:]
    q = (rmsnorm(q_lat, q_g) @ w_qb).reshape(B, N, MLA_HEADS, MLA_NOPE + MLA_ROPE)
    return q[..., :MLA_NOPE], q[..., MLA_NOPE:], ckv, kpe

def mla_expand(ckv, w_kvb):
    B, N, _ = ckv.shape
    kv = (ckv @ w_kvb).reshape(B, N, MLA_HEADS, MLA_NOPE + MLA_V)
    return kv[..., :MLA_NOPE], kv[..., MLA_NOPE:]

def block_attention(qn, qp, kn, kp, v):
    B, Nq, H, _ = qn.shape
    nb = Nq // Q_BLOCK
    qn_b = qn.reshape(B, nb, Q_BLOCK, H, MLA_NOPE).swapaxes(0, 1)
    qp_b = qp.reshape(B, nb, Q_BLOCK, H, MLA_ROPE).swapaxes(0, 1)

    def one(args):
        qnb, qpb = args
        s = (jnp.einsum("bqhd,bkhd->bhqk", qnb, kn) + jnp.einsum("bqhr,bkr->bhqk", qpb, kp))
        p = jax.nn.softmax(s.astype(jnp.float32) * ATTN_SCALE, axis=-1).astype(v.dtype)
        return jnp.einsum("bhqk,bkhd->bqhd", p, v)

    o = lax.map(one, (qn_b, qp_b))
    return o.swapaxes(0, 1).reshape(B, Nq, H * MLA_V)

def moe(h, w_router, b_router, wg, wu, wd):
    B, N, D = h.shape
    x = h.reshape(B * N, D)
    T = x.shape[0]
    scores = jax.nn.sigmoid((x @ w_router).astype(jnp.float32))
    sel = scores + b_router.astype(jnp.float32)
    gsc = jnp.sum(lax.top_k(sel.reshape(T, N_EXPERT_GROUPS, EXPERTS_PER_GROUP), 2)[0], axis=-1)
    best = jnp.argmax(gsc, axis=-1)
    in_group = (jnp.arange(N_EXPERTS) // EXPERTS_PER_GROUP)[None, :] == best[:, None]
    _, idx = lax.top_k(jnp.where(in_group, sel, -jnp.inf), TOP_K)
    w = jnp.take_along_axis(scores, idx, axis=-1)
    w = w / jnp.sum(w, axis=-1, keepdims=True)
    combine = jnp.sum(jax.nn.one_hot(idx, N_EXPERTS, dtype=jnp.float32) * w[..., None], axis=1)
    hid = jax.nn.silu(jnp.einsum("td,edf->tef", x, wg)) * jnp.einsum("td,edf->tef", x, wu)
    hid = hid * combine[..., None].astype(hid.dtype)
    y = jnp.einsum("tef,efd->td", hid, wd)
    return y.reshape(B, N, D)

def setup_inputs(seed: int = 0) -> dict:
    key = jax.random.key(seed)
    ks = jax.random.split(key, 32)
    f32 = jnp.float32

    def nrm(k, shape, scale):
        return jax.random.normal(k, shape, f32) * scale

    D = D_MODEL
    H = MLSTM_HEADS
    gate_off = jnp.array([0.0, 3.0, 0.0, 3.0], f32)[None, :, None]
    return {
        "x_prompt": nrm(ks[0], (BATCH, SEQ, D), 1.0),
        "x_sample": nrm(ks[1], (DEC_BATCH, DEC_SEQ, D), 1.0),
        "state_mlstm_C": nrm(ks[2], (DEC_BATCH, N_MLSTM_LAYERS, 2, H, MLSTM_DK, MLSTM_DV), 0.5),
        "state_mlstm_n": nrm(ks[3], (DEC_BATCH, N_MLSTM_LAYERS, 2, H, MLSTM_DK), 0.5),
        "state_mlstm_m": nrm(ks[4], (DEC_BATCH, N_MLSTM_LAYERS, 2, H), 0.5),
        "cache_mla_ckv": nrm(ks[5], (DEC_BATCH, N_MLA_LAYERS, PAST_LEN, MLA_KV_LORA), 1.0),
        "cache_mla_kpe": nrm(ks[6], (DEC_BATCH, N_MLA_LAYERS, PAST_LEN, MLA_ROPE), 1.0),
        "c": nrm(ks[7], (DEC_BATCH, D), 1.0),
        "c_ctx": nrm(ks[8], (D,), 1.0),
        "w_ada": nrm(ks[9], (DEPTH, D, 6 * D), 0.5 * D ** -0.5),
        "b_ada": nrm(ks[10], (DEPTH, 6 * D), 0.02),
        "norm_mix": 1.0 + nrm(ks[11], (DEPTH, D), 0.05),
        "norm_ffn": 1.0 + nrm(ks[12], (DEPTH, D), 0.05),
        "norm_final": 1.0 + nrm(ks[13], (D,), 0.05),
        "w_pool": nrm(ks[14], (N_POOL_LAYERS, POOL_GROUPS, POOL_GW, POOL_GW), POOL_GW ** -0.5),
        "pool_scale": 1.0 + nrm(ks[15], (N_POOL_LAYERS, D), 0.1),
        "w_mlstm_in": nrm(ks[16], (N_MLSTM_LAYERS, D, MLSTM_IN), D ** -0.5),
        "b_mlstm_gate": gate_off + nrm(ks[17], (N_MLSTM_LAYERS, 4, H), 0.1),
        "mlstm_head_g": 1.0 + nrm(ks[18], (N_MLSTM_LAYERS, H * MLSTM_DV), 0.05),
        "w_mlstm_out": nrm(ks[19], (N_MLSTM_LAYERS, H * MLSTM_DV, D), (H * MLSTM_DV) ** -0.5),
        "w_mla_in": nrm(ks[20], (N_MLA_LAYERS, D, MLA_IN), D ** -0.5),
        "mla_q_g": 1.0 + nrm(ks[21], (N_MLA_LAYERS, MLA_Q_LORA), 0.05),
        "mla_kv_g": 1.0 + nrm(ks[22], (N_MLA_LAYERS, MLA_KV_LORA), 0.05),
        "w_mla_qb": nrm(ks[23], (N_MLA_LAYERS, MLA_Q_LORA, MLA_HEADS * (MLA_NOPE + MLA_ROPE)), MLA_Q_LORA ** -0.5),
        "w_mla_kvb": nrm(ks[24], (N_MLA_LAYERS, MLA_KV_LORA, MLA_HEADS * (MLA_NOPE + MLA_V)), MLA_KV_LORA ** -0.5),
        "w_mla_out": nrm(ks[25], (N_MLA_LAYERS, MLA_HEADS * MLA_V, D), (MLA_HEADS * MLA_V) ** -0.5),
        "w_router": nrm(ks[26], (D, N_EXPERTS), D ** -0.5),
        "b_router": nrm(ks[27], (N_EXPERTS,), 0.01),
        "w_exp_gate": nrm(ks[28], (DEPTH, N_EXPERTS, D, D_EXPERT), D ** -0.5),
        "w_exp_up": nrm(ks[29], (DEPTH, N_EXPERTS, D, D_EXPERT), D ** -0.5),
        "w_exp_down": nrm(ks[30], (DEPTH, N_EXPERTS, D_EXPERT, D), D_EXPERT ** -0.5),
    }

def reference(x_prompt, x_sample, state_mlstm_C, state_mlstm_n, state_mlstm_m, cache_mla_ckv,
              cache_mla_kpe, c, c_ctx, w_ada, b_ada, norm_mix, norm_ffn, norm_final, w_pool,
              pool_scale, w_mlstm_in, b_mlstm_gate, mlstm_head_g, w_mlstm_out, w_mla_in, mla_q_g,
              mla_kv_g, w_mla_qb, w_mla_kvb, w_mla_out, w_router, b_router, w_exp_gate, w_exp_up,
              w_exp_down):
    x = x_prompt
    new_C, new_n, new_m, new_ckv, new_kpe = [], [], [], [], []
    for i in range(DEPTH):
        kind, j = i % N_MIXERS, i // N_MIXERS
        mod = ada_mod(c_ctx[None, :], w_ada[i], b_ada[i])
        h = modulate(rmsnorm(x, norm_mix[i]), mod[:, 0], mod[:, 1])
        if kind == 0:
            y = pool_mixer(h, w_pool[j], pool_scale[j])
        elif kind == 1:
            z = mlstm_zero_state(x.shape[0])
            y, st_f, st_b = mlstm_mixer(h, w_mlstm_in[j], b_mlstm_gate[j], mlstm_head_g[j],
                                        w_mlstm_out[j], z, z)
            new_C.append(jnp.stack([st_f[0], st_b[0]], axis=1))
            new_n.append(jnp.stack([st_f[1], st_b[1]], axis=1))
            new_m.append(jnp.stack([st_f[2], st_b[2]], axis=1))
        else:
            qn, qp, ckv, kpe = mla_project(h, w_mla_in[j], mla_q_g[j], mla_kv_g[j], w_mla_qb[j])
            kn, v = mla_expand(ckv, w_mla_kvb[j])
            y = block_attention(qn, qp, kn, kpe, v) @ w_mla_out[j]
            new_ckv.append(ckv)
            new_kpe.append(kpe)
        x = x + mod[:, None, 2] * y
        h = modulate(rmsnorm(x, norm_ffn[i]), mod[:, 3], mod[:, 4])
        x = x + mod[:, None, 5] * moe(h, w_router, b_router, w_exp_gate[i], w_exp_up[i], w_exp_down[i])
    y_prompt = rmsnorm(x, norm_final)
    new_state_mlstm_C = jnp.stack(new_C, axis=1)
    new_state_mlstm_n = jnp.stack(new_n, axis=1)
    new_state_mlstm_m = jnp.stack(new_m, axis=1)
    new_cache_mla_ckv = jnp.stack(new_ckv, axis=1)
    new_cache_mla_kpe = jnp.stack(new_kpe, axis=1)

    x = x_sample
    n_lat = x_sample.shape[1]
    for i in range(DEPTH):
        kind, j = i % N_MIXERS, i // N_MIXERS
        mod = ada_mod(c, w_ada[i], b_ada[i])
        h = modulate(rmsnorm(x, norm_mix[i]), mod[:, 0], mod[:, 1])
        if kind == 0:
            y = pool_mixer(h, w_pool[j], pool_scale[j])
        elif kind == 1:
            init_f = (state_mlstm_C[:, j, 0], state_mlstm_n[:, j, 0], state_mlstm_m[:, j, 0])
            init_b = (state_mlstm_C[:, j, 1], state_mlstm_n[:, j, 1], state_mlstm_m[:, j, 1])
            y, _, _ = mlstm_mixer(h, w_mlstm_in[j], b_mlstm_gate[j], mlstm_head_g[j],
                                  w_mlstm_out[j], init_f, init_b)
        else:
            qn, qp, ckv, kpe = mla_project(h, w_mla_in[j], mla_q_g[j], mla_kv_g[j], w_mla_qb[j])
            qp = rope_axial(qp, n_lat)
            kpe = rope_axial(kpe, n_lat)
            ckv_all = jnp.concatenate([cache_mla_ckv[:, j].astype(ckv.dtype), ckv], axis=1)
            kpe_all = jnp.concatenate([cache_mla_kpe[:, j].astype(kpe.dtype), kpe], axis=1)
            kn, v = mla_expand(ckv_all, w_mla_kvb[j])
            y = block_attention(qn, qp, kn, kpe_all, v) @ w_mla_out[j]
        x = x + mod[:, None, 2] * y
        h = modulate(rmsnorm(x, norm_ffn[i]), mod[:, 3], mod[:, 4])
        x = x + mod[:, None, 5] * moe(h, w_router, b_router, w_exp_gate[i], w_exp_up[i], w_exp_down[i])
    y_sample = rmsnorm(x, norm_final)
    return (y_prompt, y_sample, new_state_mlstm_C, new_state_mlstm_n, new_state_mlstm_m,
            new_cache_mla_ckv, new_cache_mla_kpe)


_drawn_inputs = setup_inputs


def setup_inputs(seed=0):
    import zlib

    import numpy as np

    out = dict(_drawn_inputs(seed))
    spreads = {}
    factors = {'state_mlstm_C': 2.676,
     'state_mlstm_n': 8.0,
     'state_mlstm_m': 3.853,
     'cache_mla_kpe': 3.232,
     'mla_q_g': 8.0}
    for name, (base, spread) in spreads.items():
        noise = np.random.default_rng([zlib.crc32(name.encode()), seed]).standard_normal(out[name].shape)
        drawn = base * np.exp(spread * noise) if base else spread * noise
        out[name] = __import__('jax').numpy.asarray(drawn.astype(out[name].dtype))
    for name, factor in factors.items():
        out[name] = (out[name] * factor).astype(out[name].dtype)
    return out
```

```python
from contextlib import ExitStack

import numpy as np

import concourse.bass as bass
from concourse import mybir

F32 = mybir.dt.float32
ALU = mybir.AluOpType
ACT = mybir.ActivationFunctionType
AX = mybir.AxisListType

P = 128
D = 1024
KC = D // P
CTX, LAT = 128, 256
TOK = CTX + LAT
NT = TOK // P
SPAN = [(0, CTX), (CTX, TOK)]
LAYERS = 4
EPS = 1e-6
WINDOWS = (2, 4, 8, 16)
PAD = 8
HP = PAD + CTX + PAD + LAT + PAD
HP_AT = [PAD, PAD + CTX + PAD]
MH, DK, DV = 4, 128, 256
AH, NOPE, ROPE, VD = 8, 128, 64, 128
QL, KVL = 512, 256
PAST = 128
KEYS = CTX + PAST + LAT
SCALE = float((NOPE + ROPE) ** -0.5)
GRID_W = 64
NE, FE = 16, 256
GROUP = 4
UNROLL = 4
UNIT = 2048
RING = 3 * UNROLL


def constants():
    s = np.arange(P)
    ident = np.eye(P, dtype=np.float32)
    mask = np.zeros((P, 2, P), np.float32)
    mask[:, 0] = np.where(s[:, None] > s[None, :], 1e30, 0.0)
    mask[:, 1] = np.where(s[:, None] < s[None, :], 1e30, 0.0)
    inv = np.zeros((len(WINDOWS), TOK), np.float32)
    for g, w in enumerate(WINDOWS):
        for a, b in SPAN:
            t = np.arange(b - a)
            inv[g, a:b] = 1.0 / (np.clip(t + w // 2, 0, b - a) - np.clip(t - w // 2, 0, b - a))
    half = ROPE // 4
    freq = np.power(np.float32(10000.0), -np.arange(half, dtype=np.float32) / half).astype(np.float32)
    pos = [np.arange(LAT) // GRID_W, np.arange(LAT) % GRID_W]
    ang = np.concatenate([np.tile(p[None, :].astype(np.float32) * freq[:, None], (2, 1)) for p in pos])
    trig = np.stack([np.tile(np.cos(ang), (2, 1)), np.tile(np.sin(ang), (2, 1))], 1).astype(np.float32)
    rot = np.zeros((P, P), np.float32)
    for m in range(P):
        if m % 32 < half:
            rot[m + half, m] = -1.0
        else:
            rot[m - half, m] = 1.0
    sel = np.zeros((MH, MH, P), np.float32)
    for h in range(MH):
        sel[h, h] = 1.0
    return {"k_ident": ident, "k_mask": mask, "k_inv": inv, "k_trig": trig, "k_rot": rot, "k_sel": sel}


def build(nc, A, O):
    ctx = ExitStack()
    with ctx:
        def sb(name, shape):
            return ctx.enter_context(nc.sbuf_tensor("sb_" + name, shape, F32))

        def sem(name):
            return ctx.enter_context(nc.semaphore(name))

        ps = [ctx.enter_context(nc.psum_tensor(f"bank{i}", [P, 512], F32)) for i in range(8)]

        xT = sb("xT", [P, KC, TOK])
        hT = sb("hT", [P, KC, TOK])
        scratch = sb("scratch", [P, KC * HP])
        ring = sb("ring", [P, RING, UNIT])
        ident = sb("ident", [P, P])
        mean_ones = sb("mean_ones", [P, P])
        ones = sb("ones", [P, P])
        trig = sb("trig", [P, 2, LAT])
        rot = sb("rot", [P, P])
        w_rt = sb("w_rt", [P, KC, NE])
        w_gt = sb("w_gt", [P, KC, 16])
        w_kp = sb("w_kp", [P, KC, ROPE])
        b_rt = sb("b_rt", [P, NE])
        b_gt = sb("b_gt", [P, 16])
        g_kv = sb("g_kv", [P, KVL])
        vecs = sb("vecs", [P, 124])
        b_ada = sb("b_ada", [P, LAYERS * 48])
        cond = sb("cond", [P, KC, 2])
        mod = sb("mod", [P, LAYERS, 48, 2])
        amp = sb("amp", [P, 2, KC, 2])
        gpool = sb("gpool", [P, KC, 2])
        rstd = sb("rstd", [P, TOK])
        m0 = sb("m0", [MH, 2])
        eps = sb("eps", [P, 1])
        acol = sb("acol", [P, 64])
        arena = sb("arena", [P, 15296])

        sq = scratch[:, 0:KC * TOK].rearrange("p (k t) -> p k t", k=KC)

        def view(off, *dims):
            n = int(np.prod(dims))
            assert off + n <= 15296, (off, dims)
            v = arena[:, off:off + n]
            if len(dims) == 2:
                v = v.rearrange("p (a b) -> p a b", a=dims[0])
            elif len(dims) == 3:
                v = v.rearrange("p (a b c) -> p a b c", a=dims[0], b=dims[1])
            elif len(dims) == 4:
                v = v.rearrange("p (a b c d) -> p a b c d", a=dims[0], b=dims[1], c=dims[2])
            return v

        x_in = view(0, NT, D)
        rows_in = view(3072, 3, P)
        hp = view(0, KC, HP)
        pong = view(KC * HP, KC, HP)
        inv = view(2 * KC * HP, 4, TOK)
        ping = scratch[:, :].rearrange("p (k t) -> p k t", k=KC)
        qT = view(0, MH, TOK)
        kT = view(1536, MH, TOK)
        VX = DV + 1
        vx = view(3072, NT, MH, VX)
        hs = view(3072 + 3084, NT, MH, DV)
        cx = view(9228, 2, MH, VX)
        hflat = hT[:, :, :].rearrange("p k t -> p (k t)")
        wgt = hflat[:, 0:1024].rearrange("p (d n) -> p d n", d=2)
        aT = hflat[:, 1024:2048].rearrange("p (d n) -> p d n", d=2)
        mm_ = hflat[:, 2048:2816].rearrange("p (d n) -> p d n", d=2)
        nd = view(11284, VX)
        p1s = view(11541, VX)
        c_st = view(11798, DV)
        mask = view(12054, 2, P)
        sel = view(12310, MH, P)[0:MH]
        kkb = view(12822, 2, P)
        n_t = view(13078, P)
        rM = view(13206, 2, TOK)[0:MH]
        rE = view(13974, 2, TOK)[0:MH]
        small = view(14742, 160)
        g_tok = small[:, 0:48].rearrange("p (t g) -> p t g", t=NT)
        rowc = small[:, 48:120].rearrange("p (d k t h) -> p d k t h", d=2, k=3, t=NT)
        ssq = small[:, 120:132]
        hrs = small[:, 132:144]
        dcol = small[:, 144:148]
        nout = small[:, 148:156]
        og = scratch[:, 0:NT * D].rearrange("p (t h d) -> p t h d", t=NT, h=MH)
        grow = view(3072 + 3084, 8, TOK)
        rI = grow[0:MH, 0:2, :]
        rB = grow[0:MH, 2:4, :]
        rA = grow[0:MH, 4:6, :]
        rS = grow[0:MH, 6:8, :]

        pl = view(0, NT, QL + KVL + ROPE)
        qlT = view(2496, QL // P, TOK)
        qpT = view(4032, AH // 2, TOK)
        knT = view(5568, AH, KEYS)
        vt = view(9664, KEYS // P, AH, VD)
        ckT = view(13760, KVL // P, KEYS)
        kpT = view(14784, KEYS)
        qnT = scratch[:, 0:AH * TOK].rearrange("p (h t) -> p h t", h=AH)
        pr = view(0, 2, TOK)
        prT = view(768, 896)
        t_rot = view(1664, LAT)
        t_cos = view(1920, LAT)
        cache = hT[:, 0, 0:KVL]
        kp2 = hT[:, 1:3, :].rearrange("p a t -> p (a t)")[:, 0:512].rearrange("p (t r) -> p t r", t=4)

        yacc = view(0, KC, TOK)
        hid = view(3072, 2, TOK)
        sg = view(3840, 2, TOK)
        combT = view(4608, TOK)
        comb_row = view(4992, NE, TOK)
        rt = view(11136, 40, NT * 16)

        const_in = sem("const_in"); x_loaded = sem("x_loaded"); rows_loaded = sem("rows_loaded")
        pool_set = sem("pool_set"); vec_t = sem("vec_t"); vec_cols = sem("vec_cols")
        xt_full = sem("xt_full"); x_ready = sem("x_ready"); cond_ready = sem("cond_ready")
        slot_in = [sem(f"slot_in{i}") for i in range(RING)]
        ada_full = sem("ada_full"); mod_ready = sem("mod_ready"); ada_unit = sem("ada_unit")
        sq_ready = sem("sq_ready"); ms_full = sem("ms_full"); rstd_ready = sem("rstd_ready")
        h_scaled = sem("h_scaled"); h_ready = sem("h_ready")
        act_step = sem("act_step"); vec_step = sem("vec_step")
        y_full = sem("y_full")
        inv_in = sem("inv_in"); pads_set = sem("pads_set"); pooled = sem("pooled")
        gate_full = sem("gate_full"); gate_tok = sem("gate_tok"); grow_full = sem("grow_full")
        rows_done = sem("rows_done"); rowc_full = sem("rowc_full"); rowc_ready = sem("rowc_ready")
        qk_full = sem("qk_full"); qk_ready = sem("qk_ready"); v_full = sem("v_full"); v_ready = sem("v_ready")
        o_full = sem("o_full"); o_ready = sem("o_ready"); state_in = sem("state_in"); state_set = sem("state_set")
        s_full = sem("s_full"); mbc_full = sem("mbc_full"); mm_ready = sem("mm_ready")
        w_ready = sem("w_ready"); at_ready = sem("at_ready"); kk_ready = sem("kk_ready")
        c_full = sem("c_full"); c_copied = sem("c_copied"); p_full = sem("p_full"); p1_ready = sem("p1_ready")
        p_used = sem("p_used"); softplus = sem("softplus")
        ss_ready = sem("ss_ready"); hrs_ready = sem("hrs_ready"); hn_ready = sem("hn_ready")
        hsT_full = sem("hsT_full"); hsT_ready = sem("hsT_ready"); nt_full = sem("nt_full"); n_copied = sem("n_copied"); rowc_set = sem("rowc_set"); vx_ones = sem("vx_ones"); tables_in = sem("tables_in")
        out_c = sem("out_c"); out_n = sem("out_n"); out_m = sem("out_m"); l_ready = sem("l_ready")
        pl_full = sem("pl_full"); pl_ready = sem("pl_ready"); pn_ready = sem("pn_ready"); prs_ready = sem("prs_ready")
        cache_in = sem("cache_in"); kp_dup = sem("kp_dup"); ql_full = sem("ql_full"); ql_ready = sem("ql_ready")
        ck_full = sem("ck_full"); ck_ready = sem("ck_ready"); kp_full = sem("kp_full"); kp_ready = sem("kp_ready")
        rot_full = sem("rot_full"); rope_ready = sem("rope_ready"); qn_full = sem("qn_full"); qn_ready = sem("qn_ready")
        qp_full = sem("qp_full"); qp_raw = sem("qp_raw"); kn_full = sem("kn_full"); kn_ready = sem("kn_ready")
        vt_full = sem("vt_full"); vt_ready = sem("vt_ready"); sc_full = sem("sc_full"); mx_ready = sem("mx_ready")
        e_ready = sem("e_ready"); p_ready = sem("p_ready"); pt_full = sem("pt_full"); pt_ready = sem("pt_ready")
        o_att = sem("o_att"); oT_ready = sem("oT_ready"); out_kv = sem("out_kv")
        rt_full = sem("rt_full"); rt_e = sem("rt_e"); comb_tok = sem("comb_tok"); combT_full = sem("combT_full")
        combT_ready = sem("combT_ready"); comb_rows = sem("comb_rows"); yacc_zero = sem("yacc_zero")
        gu_full = sem("gu_full"); cb_full = sem("cb_full"); sg_exp = sem("sg_exp"); hid_ready = sem("hid_ready")
        yp_full = sem("yp_full"); yp_used = sem("yp_used")
        yt_full = sem("yt_full"); yt_ready = sem("yt_ready"); out_y = sem("out_y")

        NCONST = 10

        units = []

        def slot(u):
            return ring[:, u % RING, :]

        def add(src, cols, release):
            units.append((src, cols, release))

        def ada_units(L, lo, hi):
            for i in range(lo, hi):
                add((A["w_ada"][L, :, i * 256:(i + 1) * 256], KC, 256), KC * 256, (ada_unit, 24 * L + i + 1))

        n_y = 0
        moe_first = []
        ada_units(0, 0, 24)
        for L in range(LAYERS):
            kind, j = L % 3, L // 3
            if L + 1 < LAYERS:
                ada_units(L + 1, 0, 12)
            if kind == 0:
                add((A["w_pool"][j].rearrange("g c d -> (g c) d"), KC, 256), KC * 256, (y_full, n_y + 8))
            elif kind == 1:
                w = A["w_mlstm_in"][j]
                for i in range(4):
                    add((w[:, i * 256:(i + 1) * 256], KC, 256), 2048, (qk_full, 2 * (i + 1)))
                for i in range(4):
                    add((w[:, 1024 + i * 256:1024 + (i + 1) * 256], KC, 256), 2048, (v_full, NT * (i + 1)))
                for i in range(4):
                    add((w[:, 2048 + i * 256:2048 + (i + 1) * 256], KC, 256), 2048, (o_full, NT * (i + 1)))
                for i in range(4):
                    add((A["w_mlstm_out"][j][:, i * 256:(i + 1) * 256], KC, 256), 2048, (y_full, n_y + 2 * (i + 1)))
            else:
                w = A["w_mla_in"][j]
                for i in range(3):
                    add((w[:, i * 256:(i + 1) * 256], KC, 256), 2048, (pl_full, NT * (i + 1)))
                for i in range(4):
                    add((A["w_mla_qb"][j][:, i * 384:(i + 1) * 384], QL // P, 384), 1536, (qp_full, i + 1))
                for i in range(2):
                    add((A["w_mla_kvb"][j][:, i * 1024:(i + 1) * 1024], KVL // P, 1024), 2048, (vt_full, 4 * (i + 1)))
                for i in range(4):
                    add((A["w_mla_out"][j][:, i * 256:(i + 1) * 256], KC, 256), 2048, (y_full, n_y + 2 * (i + 1)))
            n_y += 8
            if L + 1 < LAYERS:
                ada_units(L + 1, 12, 24)
            moe_first.append(len(units))
            for e in range(NE):
                g = NE * L + e
                for n, name in enumerate(("w_exp_gate", "w_exp_up")):
                    add((A[name][L, e], KC, 256), 2048, (gu_full, 4 * g + 2 * (n + 1)))
                add((A["w_exp_down"][L, e], FE // P, D), 2048, (yp_full, 8 * (g + 1)))

        def arrived(eng, u):
            eng.wait_ge(slot_in[u % RING], 16 * (u // RING + 1))

        block = ctx.enter_context(nc.Block())

        @block.sync
        def _(sp):
            def load(u):
                src, n, _ = units[u]
                ap, k, c = src
                if u >= RING:
                    s, value = units[u - RING][2]
                    sp.wait_ge(s, value)
                sp.dma_start(slot(u)[:, 0:n].rearrange("p (k n) -> p k n", k=k),
                             ap.rearrange("(k p) n -> p k n", p=P)).then_inc(slot_in[u % RING], 16)

            u = 0
            for L in range(LAYERS):
                first = moe_first[L]
                while u < first + RING:
                    load(u)
                    u += 1
                with sp.Fori(1, NE // UNROLL) as it:
                    for b in range(RING):
                        _, _, (s, value) = units[first + b]
                        e = it * UNROLL + b // 3
                        name = ("w_exp_gate", "w_exp_up", "w_exp_down")[b % 3]
                        step = 8 * UNROLL if b % 3 == 2 else 4 * UNROLL
                        sp.wait_ge(s, (it - 1) * step + value)
                        k = KC if b % 3 < 2 else FE // P
                        sp.dma_start(slot(first + b).rearrange("p (k n) -> p k n", k=k),
                                     A[name][L, bass.ds(e, 1)].rearrange("e (k p) n -> p (e k) n", p=P))\
                          .then_inc(slot_in[(first + b) % RING], 16)
                u = first + 3 * NE
            assert u == len(units)

        @block.tensor
        def _(pe):
            def mm(out, lhsT, rhs, first, last):
                return pe.matmul(out, lhsT, rhs, start=first, stop=last)

            state = {"u": 0}

            def take():
                u = state["u"]
                state["u"] = u + 1
                arrived(pe, u)
                return slot(u)

            def ada(L, lo, hi):
                if lo == 0:
                    pe.wait_ge(cond_ready, 2)
                    if L:
                        pe.wait_ge(mod_ready, L)
                for i in range(lo, hi):
                    w = take().rearrange("p (k n) -> p k n", k=KC)
                    for b in range(2):
                        c = 2 * (2 * i + b)
                        for k in range(KC):
                            ins = mm(ps[7][:, c:c + 2], w[:, k, b * P:(b + 1) * P], cond[:, k, :], k == 0, k == KC - 1)
                    ins.then_inc(ada_unit, 1)

            def norm(n):
                for k in range(KC):
                    if k % 2 == 0:
                        pe.wait_ge(sq_ready, 4 * n + k // 2 + 1)
                    ins = mm(ps[6][:, 0:TOK], mean_ones[:, :], sq[:, k, :], k == 0, k == KC - 1)
                ins.then_inc(ms_full, 1)

            def project(r, src, ready, n_src):
                for i in range(4):
                    w = take().rearrange("p (k n) -> p k n", k=KC)
                    for b in range(2):
                        c = 2 * i + b
                        if c >= 4:
                            pe.wait_ge(x_ready, 8 * (r + 1) + c - 3)
                        for k in range(KC):
                            if c == 0:
                                pe.wait_ge(ready, n_src[k])
                            ins = mm(ps[c % 4][:, 0:TOK], w[:, k, b * P:(b + 1) * P], src[:, k, :], k == 0, k == KC - 1)
                        ins.then_inc(y_full, 1)

            def pool_mixer(r):
                w = take().rearrange("p (k n) -> p k n", k=KC)
                for c in range(KC):
                    g = c // 2
                    pe.wait_ge(pooled, 4 * (0 if r == 0 else 1) + g + 1)
                    if c >= 4:
                        pe.wait_ge(x_ready, 8 * (r + 1) + c - 3)
                    for k in range(2):
                        ins = mm(ps[c % 4][:, 0:TOK], w[:, 2 * g + k, (c % 2) * P:(c % 2 + 1) * P],
                                 hT[:, 2 * g + k, :], k == 0, k == 1)
                    ins.then_inc(y_full, 1)

            def mlstm(r):
                pe.wait_ge(h_ready, 16 * (r + 1))
                for t in range(NT):
                    for k in range(KC):
                        ins = mm(ps[4][:, t * 16:(t + 1) * 16], hT[:, k, t * P:(t + 1) * P], w_gt[:, k, :], k == 0, k == KC - 1)
                ins.then_inc(gate_full, 1)
                pe.wait_ge(gate_tok, 1)
                for g in range(4):
                    for t in range(NT):
                        ins = pe.transpose(ps[g][0:MH, t * P:(t + 1) * P], g_tok[:, t, g * 4:(g + 1) * 4], ident[:, :])
                ins.then_inc(grow_full, 1)
                for i in range(4):
                    w = take().rearrange("p (k n) -> p k n", k=KC)
                    for b in range(2):
                        c = 2 * i + b
                        if c >= 2:
                            pe.wait_ge(qk_ready, c - 1)
                        for k in range(KC):
                            ins = mm(ps[5 + c % 2][:, 0:TOK], w[:, k, b * P:(b + 1) * P], hT[:, k, :], k == 0, k == KC - 1)
                        ins.then_inc(qk_full, 1)
                for i in range(4):
                    w = take().rearrange("p (k n) -> p k n", k=KC)
                    for t in range(NT):
                        c = NT * i + t
                        if c >= 2:
                            pe.wait_ge(v_ready, c - 1)
                        else:
                            pe.wait_ge(qk_ready, 7 + c)
                        for k in range(KC):
                            ins = mm(ps[5 + c % 2][:, 0:DV], hT[:, k, t * P:(t + 1) * P], w[:, k, :], k == 0, k == KC - 1)
                        ins.then_inc(v_full, 1)
                pe.wait_ge(rows_done, 1)
                for d in range(2):
                    for q, src in enumerate((rA, rS, rE)):
                        for t in range(NT):
                            c = ((d * 3 + q) * NT + t) * MH
                            ins = pe.transpose(ps[4][:, 64 + c:64 + c + MH], src[:, d, t * P:(t + 1) * P], ident[0:MH, 0:MH])
                ins.then_inc(rowc_full, 1)
                for i in range(4):
                    w = take().rearrange("p (k n) -> p k n", k=KC)
                    for t in range(NT):
                        c = NT * i + t
                        pe.wait_ge(*((l_ready, c - 1) if c >= 2 else (v_ready, 11 + c)))
                        for k in range(KC):
                            ins = mm(ps[5 + c % 2][:, 0:DV], hT[:, k, t * P:(t + 1) * P], w[:, k, :], k == 0, k == KC - 1)
                        ins.then_inc(o_full, 1)
                pe.wait_ge(rowc_ready, 1)
                pe.wait_ge(state_set, 1)
                pe.wait_ge(state_in, 32)
                pe.wait_ge(vx_ones, 1)
                pe.wait_ge(tables_in, 32)
                pe.wait_ge(l_ready, 12)
                npj = 0
                for h in range(MH):
                    if h:
                        pe.wait_ge(at_ready, 3 * h)
                        pe.wait_ge(kk_ready, 2 * h)
                    for c, (s, t) in enumerate(((0, 0), (1, 1), (2, 2), (1, 2))):
                        mm(ps[0][:, c * P:(c + 1) * P], kT[:, h, s * P:(s + 1) * P], qT[:, h, t * P:(t + 1) * P], True, True)
                    mm(ps[1][:, 0:P], kT[:, h, 2 * P:3 * P], qT[:, h, P:2 * P], True, True)
                    pe.transpose(ps[1][:, P:2 * P], kT[:, h, 0:P], ident[:, :]).then_inc(s_full, 1)
                    for d in range(2):
                        if h:
                            pe.wait_ge(w_ready, 2 * (h - 1) + d + 1)
                        mm(ps[2 + d][:, 0:TOK], sel[:, h, :], rM[:, d, :], True, True).then_inc(mbc_full, 1)
                    for d in range(2):
                        if npj >= 3:
                            pe.wait_ge(p_used, npj - 2)
                        pe.wait_ge(kk_ready, 2 * h + d + 1)
                        mm(ps[4 + npj % 3][:, 0:VX], kkb[:, d, :], vx[:, 0, h, :], True, True).then_inc(p_full, 1)
                        npj += 1
                        pe.wait_ge(at_ready, 3 * h + (1 if d == 0 else 3))
                        for t in range(NT):
                            if npj >= 3:
                                pe.wait_ge(p_used, npj - 2)
                            b = ps[4 + npj % 3][:, 0:VX]
                            if t == 0 or (t == 1 and d == 0) or (t == 2 and d == 1):
                                mm(b, aT[:, d, t * P:(t + 1) * P], vx[:, t, h, :], True, True).then_inc(p_full, 1)
                            else:
                                mm(b, aT[:, d, t * P:(t + 1) * P], vx[:, t, h, :], True, False)
                                o = 2 if t == 1 else 1
                                mm(b, aT[:, d, 3 * P:4 * P], vx[:, o, h, :], False, True).then_inc(p_full, 1)
                            npj += 1
                            if t:
                                if npj >= 3:
                                    pe.wait_ge(p_used, npj - 2)
                                mm(ps[4 + npj % 3][:, 0:VX], qT[:, h, t * P:(t + 1) * P], cx[:, d, h, :], True, True)\
                                    .then_inc(p_full, 1)
                                npj += 1
                pe.wait_ge(p_used, npj)
                pe.transpose(ps[2][0:8, 0:P], nout, ident[:, :]).then_inc(nt_full, 1)
                pe.wait_ge(hn_ready, 12)
                for c in range(KC):
                    if c >= 2:
                        pe.wait_ge(hsT_ready, c - 1)
                    for t in range(NT):
                        ins = pe.transpose(ps[c % 2][:, t * P:(t + 1) * P],
                                           hs[:, t, c // 2, (c % 2) * P:(c % 2 + 1) * P], ident[:, :])
                    ins.then_inc(hsT_full, 1)
                pe.wait_ge(hsT_ready, 8)
                pe.wait_ge(n_copied, 1)
                project(r, hT, hsT_ready, [8] * KC)

            def mla(r):
                pe.wait_ge(h_ready, 16 * (r + 1))
                for i in range(4):
                    if i < 3:
                        w = take().rearrange("p (k n) -> p k n", k=KC)
                    else:
                        w = w_kp
                    n = 256 if i < 3 else ROPE
                    for t in range(NT):
                        c = NT * i + t
                        if c >= 4:
                            pe.wait_ge(pl_ready, c - 3)
                        for k in range(KC):
                            ins = mm(ps[c % 4][:, 0:n], hT[:, k, t * P:(t + 1) * P], w[:, k, :], k == 0, k == KC - 1)
                        ins.then_inc(pl_full, 1)
                pe.wait_ge(pn_ready, 3)
                pe.wait_ge(pl_ready, 12)
                for c in range(4):
                    for t in range(NT):
                        ins = pe.transpose(ps[c][:, t * P:(t + 1) * P], pl[:, t, c * P:(c + 1) * P], ident[:, :])
                    ins.then_inc(ql_full, 1)
                pe.wait_ge(pn_ready, 6)
                pe.wait_ge(cache_in, 48)
                for c in range(2):
                    for s in range(4):
                        src = cache[:, c * P:(c + 1) * P] if s == 1 else \
                            pl[:, max(s - 1, 0), QL + c * P:QL + (c + 1) * P]
                        ins = pe.transpose(ps[4 + c][:, s * P:(s + 1) * P], src, ident[:, :])
                    ins.then_inc(ck_full, 1)
                pe.wait_ge(kp_dup, 1)
                for s in range(4):
                    ins = pe.transpose(ps[6][:, s * P:(s + 1) * P], kp2[:, s, :], ident[:, :])
                ins.then_inc(kp_full, 1)
                pe.wait_ge(kp_ready, 1)
                pe.wait_ge(ql_ready, 4)
                mm(ps[6][:, 0:LAT], rot[:, :], kpT[:, KEYS - LAT:KEYS], True, True).then_inc(rot_full, 1)
                nq = 0
                for i in range(4):
                    w = take()[:, 0:1536].rearrange("p (k n) -> p k n", k=4)
                    for b in range(3):
                        if nq >= 4:
                            if (nq - 4) % 3 == 2:
                                pe.wait_ge(qp_raw, (nq - 4) // 3 + 1)
                            else:
                                pe.wait_ge(qn_ready, (nq - 4) // 3 * 2 + (nq - 4) % 3 + 1)
                        bank = ps[nq % 4][:, 0:TOK]
                        if b < 2:
                            for k in range(4):
                                ins = mm(bank, w[:, k, b * 192:b * 192 + NOPE], qlT[:, k, :], k == 0, k == 3)
                        else:
                            for o in range(2):
                                for k in range(4):
                                    ins = mm(bank[o * ROPE:(o + 1) * ROPE, :], w[:, k, o * 192 + NOPE:(o + 1) * 192],
                                             qlT[:, k, :], k == 0, k == 3)
                        ins.then_inc(qn_full if b < 2 else qp_full, 1)
                        nq += 1
                for i in range(4):
                    pe.wait_ge(qp_raw, i + 1)
                    pe.wait_ge(rope_ready, i + 1)
                    mm(ps[6][:, 0:LAT], rot[:, :], qpT[:, i, CTX:TOK], True, True).then_inc(rot_full, 1)
                pe.wait_ge(ck_ready, 2)
                for i in range(2):
                    w = take().rearrange("p (k n) -> p k n", k=2)
                    for b in range(4):
                        h = 4 * i + b
                        if h >= 2:
                            pe.wait_ge(kn_ready, h - 1)
                        else:
                            pe.wait_ge(qn_ready, 8)
                        for k in range(2):
                            ins = mm(ps[4 + h % 2][:, :], w[:, k, b * 256:b * 256 + NOPE], ckT[:, k, :], k == 0, k == 1)
                        ins.then_inc(kn_full, 1)
                    for s in range(4):
                        c = 4 * i + s
                        if c >= 4:
                            pe.wait_ge(vt_ready, c - 3)
                        else:
                            pe.wait_ge(qp_raw, 4)
                        for k in range(2):
                            rhs = w[:, k, :].rearrange("p (h n) -> p h n", h=4)[:, :, NOPE:]
                            ins = mm(ps[c % 4][:, :].rearrange("p (h n) -> p h n", h=4), ckT[:, k, s * P:(s + 1) * P],
                                     rhs, k == 0, k == 1)
                        ins.then_inc(vt_full, 1)
                pe.wait_ge(kn_ready, 8)
                pe.wait_ge(vt_ready, 8)
                pe.wait_ge(rope_ready, 5)
                def scores(h, t):
                    c = NT * h + t
                    if c >= 3:
                        pe.wait_ge(e_ready, c - 2)
                    lo, hi = (0, CTX) if t == 0 else (CTX, KEYS)
                    b = ps[c % 3][:, 0:hi - lo]
                    o = (h % 2) * ROPE
                    mm(b, qnT[:, h, t * P:(t + 1) * P], knT[:, h, lo:hi], True, False)
                    mm(b, qpT[o:o + ROPE, h // 2, t * P:(t + 1) * P], kpT[o:o + ROPE, lo:hi], False, True)\
                        .then_inc(sc_full, 1)

                for t in range(NT):
                    scores(0, t)
                for h in range(AH):
                    for t in range(NT):
                        c = NT * h + t
                        pe.wait_ge(p_ready, c + 1)
                        if h and t == 0:
                            pe.wait_ge(pt_ready, 2 * h)
                        if t == 0:
                            ins = pe.transpose(ps[4][:, 256:384], pr[:, c % 2, 0:P], ident[:, :])
                        else:
                            for s in range(3):
                                bank, o = (ps[3], s * 256) if s < 2 else (ps[4], 0)
                                ins = pe.transpose(bank[:, o + (t - 1) * P:o + t * P], pr[:, c % 2, s * P:(s + 1) * P], ident[:, :])
                        ins.then_inc(pt_full, 1)
                        if h + 1 < AH:
                            scores(h + 1, t)
                    pe.wait_ge(pt_ready, 2 * (h + 1))
                    if h >= 2:
                        pe.wait_ge(oT_ready, h - 1)
                    b = ps[5 + h % 2]
                    mm(b[:, 0:CTX], vt[:, 0, h, :], prT[:, 768:896], True, True)
                    for s in range(3):
                        ins = mm(b[:, CTX:TOK], vt[:, 1 + s, h, :], prT[:, s * 256:(s + 1) * 256], s == 0, s == 2)
                    ins.then_inc(o_att, 1)
                pe.wait_ge(oT_ready, 8)
                project(r, hT, oT_ready, [8] * KC)

            def experts(L, n):
                pe.wait_ge(h_ready, 16 * (n + 1))
                for t in range(NT):
                    for k in range(KC):
                        ins = mm(ps[5][:, t * 16:(t + 1) * 16], hT[:, k, t * P:(t + 1) * P], w_rt[:, k, :], k == 0, k == KC - 1)
                ins.then_inc(rt_full, 1)
                if L + 1 < LAYERS:
                    ada(L + 1, 12, 24)
                pe.wait_ge(comb_tok, L + 1)
                for t in range(NT):
                    ins = pe.transpose(ps[5][0:NE, 64 + t * P:64 + (t + 1) * P], rt[:, 0, t * 16:(t + 1) * 16], ident[:, :])
                ins.then_inc(combT_full, 1)
                u0 = state["u"]
                turns = 3 * NE // RING
                assert u0 == moe_first[L]
                pe.wait_ge(comb_rows, 16 * (L + 1))
                with pe.Fori(0, turns) as it:
                    for b in range(UNROLL):
                        g = NE * L + b
                        uu = u0 + 3 * b
                        for half in range(2):
                            u = uu + half
                            pe.wait_ge(slot_in[u % RING], it * 16 + 16 * (u // RING + 1))
                            w = slot(u).rearrange("p (k n) -> p k n", k=KC)
                            for f in range(2):
                                for k in range(KC):
                                    ins = mm(ps[2 * half + f][:, 0:TOK], w[:, k, f * P:(f + 1) * P], hT[:, k, :], k == 0, k == KC - 1)
                                ins.then_inc(gu_full, 1)
                        e = it * UNROLL + b
                        pe.matmul(ps[4][:, 0:TOK], ones[0:1, :], comb_row[0:1, bass.ds(e, 1), :].rearrange("p e t -> p (e t)"),
                                  start=True, stop=True).then_inc(cb_full, 1)
                        u = uu + 2
                        pe.wait_ge(slot_in[u % RING], it * 16 + 16 * (u // RING + 1))
                        w = slot(u).rearrange("p (k n) -> p k n", k=2)
                        pe.wait_ge(hid_ready, it * (2 * UNROLL) + 2 * (g + 1))
                        for c in range(KC):
                            if c >= 2:
                                pe.wait_ge(yp_used, it * (8 * UNROLL) + 8 * g + c - 1)
                            for f in range(2):
                                ins = mm(ps[5 + c % 2][:, 0:TOK], w[:, f, c * P:(c + 1) * P], hid[:, f, :], f == 0, f == 1)
                            ins.then_inc(yp_full, 1)
                state["u"] = u0 + 3 * NE

            pe.wait_ge(const_in, 16 * NCONST)
            pe.wait_ge(rows_loaded, 160)
            pe.wait_ge(pool_set, 3)
            pe.transpose(ps[6][:, 0:124], rows_in[0:124, 0, :], ident[0:124, 0:124])
            pe.transpose(ps[6][:, 128:224], rows_in[0:96, 1, :], ident[0:96, 0:96])
            pe.transpose(ps[6][:, 256:352], rows_in[0:96, 2, :], ident[0:96, 0:96]).then_inc(vec_t, 1)
            pe.wait_ge(x_loaded, 16 * NT)
            for c in range(KC):
                if c >= 4:
                    pe.wait_ge(x_ready, c - 3)
                for t in range(NT):
                    ins = pe.transpose(ps[c % 4][:, t * P:(t + 1) * P], x_in[:, t, c * P:(c + 1) * P], ident[:, :])
                ins.then_inc(xt_full, 1)
            pe.wait_ge(vec_cols, 3)
            ada(0, 0, 24)
            for L in range(LAYERS):
                norm(2 * L)
                if L + 1 < LAYERS:
                    ada(L + 1, 0, 12)
                (pool_mixer, mlstm, mla)[L % 3](2 * L)
                norm(2 * L + 1)
                experts(L, 2 * L + 1)
            norm(2 * LAYERS)
            for t in range(NT):
                for half in range(2):
                    c = 2 * t + half
                    pe.wait_ge(h_scaled, 16 * (2 * LAYERS + 1))
                    if c >= 4:
                        pe.wait_ge(yt_ready, c - 3)
                    for k in range(4):
                        ins = pe.transpose(ps[c % 4][:, k * P:(k + 1) * P], hT[:, 4 * half + k, t * P:(t + 1) * P], ident[:, :])
                    ins.then_inc(yt_full, 1)

        @block.scalar
        def _(act):
            n_step = {"n": 0}

            def step(ins):
                ins.then_inc(act_step, 1)
                n_step["n"] += 1

            def settle():
                act.wait_ge(act_step, n_step["n"])

            act.dma_start(ident[:, :], A["k_ident"]).then_inc(const_in, 16)
            act.dma_start(rows_in[0:8, 0, :], A["c_ctx"].rearrange("(r n) -> r n", n=P)).then_inc(rows_loaded, 16)
            act.dma_start(rows_in[8:16, 0, :], A["c"].rearrange("a (r n) -> (a r) n", n=P)).then_inc(rows_loaded, 16)
            act.dma_start(rows_in[16:48, 0, :], A["norm_mix"].rearrange("l (r n) -> (l r) n", n=P)).then_inc(rows_loaded, 16)
            act.dma_start(rows_in[48:80, 0, :], A["norm_ffn"].rearrange("l (r n) -> (l r) n", n=P)).then_inc(rows_loaded, 16)
            act.dma_start(rows_in[80:88, 0, :], A["norm_final"].rearrange("(r n) -> r n", n=P)).then_inc(rows_loaded, 16)
            act.dma_start(rows_in[88:104, 0, :], A["pool_scale"].rearrange("l (r n) -> (l r) n", n=P)).then_inc(rows_loaded, 16)
            act.dma_start(rows_in[104:112, 0, :], A["mlstm_head_g"].rearrange("l (r n) -> (l r) n", n=P)).then_inc(rows_loaded, 16)
            act.dma_start(rows_in[112:116, 0, :], A["mla_q_g"].rearrange("l (r n) -> (l r) n", n=P)).then_inc(rows_loaded, 16)
            act.dma_start(rows_in[116:124, 0, :], A["state_mlstm_n"].rearrange("b l s h k -> (b l s h) k")).then_inc(rows_loaded, 16)
            act.dma_start(rows_in[0:96, 1:3, :],
                          A["b_ada"].rearrange("l (r n) -> (l r) n", n=P).rearrange("(a r) n -> r a n", a=2)).then_inc(rows_loaded, 16)
            for t in range(NT):
                src = A["x_prompt"][0] if t == 0 else A["x_sample"][0, (t - 1) * P:t * P]
                act.dma_start(x_in[:, t, :], src).then_inc(x_loaded, 16)
            act.dma_start(trig[:, :, :], A["k_trig"]).then_inc(const_in, 16)
            act.dma_start(rot[:, :], A["k_rot"]).then_inc(const_in, 16)
            act.dma_start(w_rt[:, :, :], A["w_router"].rearrange("(k p) n -> p k n", p=P)).then_inc(const_in, 16)
            act.dma_start(w_gt[:, :, :], A["w_mlstm_in"][0, :, 3072:3088].rearrange("(k p) n -> p k n", p=P)).then_inc(const_in, 16)
            act.dma_start(w_kp[:, :, :], A["w_mla_in"][0, :, 768:832].rearrange("(k p) n -> p k n", p=P)).then_inc(const_in, 16)
            act.dma_start(b_rt[:, :], A["b_router"].partition_broadcast(P)).then_inc(const_in, 16)
            act.dma_start(b_gt[:, :], A["b_mlstm_gate"].rearrange("l a h -> (l a h)").partition_broadcast(P)).then_inc(const_in, 16)
            act.dma_start(g_kv[:, :], A["mla_kv_g"][0].partition_broadcast(P)).then_inc(const_in, 16)
            with nc.allow_non_contiguous_dma(reason="eight floats"):
                act.dma_start(m0[:, :], A["state_mlstm_m"].rearrange("b l s h -> h (b l s)")).then_inc(const_in, 16)

            act.wait_ge(vec_cols, 1)
            cc = vecs[:, 0:16].rearrange("p (c k) -> p k c", c=2)
            act.wait_ge(const_in, 16 * NCONST)
            act.activation(cond[:, :, :], cc, ACT.Exp, scale=-1.0).then_inc(cond_ready, 1)

            def norm(n, bias, out):
                for k in range(4):
                    act.wait_ge(x_ready, 8 * (n + 1) - 6 + 2 * k)
                    if n:
                        act.wait_ge(ms_full, n)
                    act.activation(sq[:, 2 * k:2 * k + 2, :], xT[:, 2 * k:2 * k + 2, :], ACT.Square).then_inc(sq_ready, 1)
                act.wait_ge(ms_full, n + 1)
                if n:
                    act.wait_ge(h_scaled, 16 * n)
                step(act.activation(rstd[:, :], ps[6][:, 0:TOK], ACT.Ln, bias=eps[:, 0:1]))
                settle()
                act.activation(rstd[:, :], rstd[:, :], ACT.Exp, scale=-0.5).then_inc(rstd_ready, 1)
                if bias is None:
                    return
                for k in range(KC):
                    for c in range(2):
                        act.wait_ge(h_scaled, 16 * n + 2 * k + c + 1)
                        o = out(k, c)
                        act.activation(o, hT[:, k, SPAN[c][0]:SPAN[c][1]], ACT.Identity, bias=bias[:, k, c:c + 1]).then_inc(h_ready, 1)

            def h_out(k, c):
                return hT[:, k, SPAN[c][0]:SPAN[c][1]]

            def hp_out(k, c):
                return hp[:, k, HP_AT[c]:HP_AT[c] + SPAN[c][1] - SPAN[c][0]]

            def mlstm(r):
                act.wait_ge(grow_full, 1)
                for d in range(2):
                    step(act.activation(rB[:, d, :], ps[2 * d + 1][0:MH, 0:TOK], ACT.Abs))
                settle()
                step(act.activation(rB, rB, ACT.Exp, scale=-1.0))
                settle()
                act.activation(rI, rB, ACT.Ln, bias=1.0).then_inc(softplus, 1)
                for c in range(8):
                    act.wait_ge(qk_full, c + 1)
                    dst = (qT if c < 4 else kT)[:, c % 4, :]
                    act.activation(dst, ps[5 + c % 2][:, 0:TOK], ACT.Copy, scale=float(DK ** -0.5) if c < 4 else 1.0).then_inc(qk_ready, 1)
                for c in range(12):
                    act.wait_ge(v_full, c + 1)
                    act.activation(vx[:, c % 3, c // 3, 0:DV], ps[5 + c % 2][:, 0:DV], ACT.Copy).then_inc(v_ready, 1)
                for c in range(12):
                    act.wait_ge(o_full, c + 1)
                    act.activation(og[:, c % 3, c // 3, :], ps[5 + c % 2][:, 0:DV], ACT.Exp, scale=-1.0).then_inc(l_ready, 1)
                act.wait_ge(rowc_set, 1)
                rc = small[:, 48:120].rearrange("p (d n) -> p d n", d=2)[:, :, 12:36]
                act.activation(rc, rc, ACT.Exp, scale=-1.0).then_inc(rowc_ready, 1)
                act.wait_ge(rowc_ready, 1)
                last_p1 = 0
                npj = 0
                for h in range(MH):
                    for d in range(2):
                        act.wait_ge(mm_ready, 2 * h + d + 1)
                        if h:
                            act.wait_ge(at_ready, 3 * h)
                            act.wait_ge(kk_ready, 2 * h)
                        for s in range(NT):
                            act.activation(wgt[:, d, s * P:(s + 1) * P], mm_[:, d, s * P:(s + 1) * P], ACT.Exp, scale=-1.0,
                                           bias=rowc[:, d, 0, s, h:h + 1])
                        s, t = (1, 2) if d == 0 else (2, 1)
                        act.activation(wgt[:, d, 3 * P:4 * P], ps[2 + d][:, t * P:(t + 1) * P], ACT.Exp, scale=-1.0,
                                       bias=rowc[:, d, 0, s, h:h + 1]).then_inc(w_ready, 1)
                    for d in range(2):
                        npj += 1
                        for t in range(NT):
                            npj += 1
                            if t:
                                npj += 1
                                act.wait_ge(p_full, npj)
                                if last_p1:
                                    act.wait_ge(p_used, last_p1)
                                last_p1 = npj
                                act.activation(p1s, ps[4 + (npj - 1) % 3][:, 0:VX], ACT.Copy, scale=rowc[:, d, 1, t, h:h + 1])\
                                   .then_inc(p1_ready, 1)
                for h in range(MH):
                    for t in range(NT):
                        act.wait_ge(ss_ready, 12)
                        act.activation(mm_[:, 0, 0:DV], hs[:, t, h, :], ACT.Square,
                                       accum_out=ssq[:, NT * h + t:NT * h + t + 1]).then_inc(act_step, 1)
                        n_step["n"] += 1
                        settle()
                step(act.activation(hrs, ssq, ACT.Ln, scale=1.0 / DV, bias=eps[:, 0:1]))
                settle()
                act.activation(hrs, hrs, ACT.Exp, scale=-0.5).then_inc(hrs_ready, 1)
                for c in range(KC):
                    act.wait_ge(hsT_full, c + 1)
                    act.activation(hT[:, c, :], ps[c % 2][:, 0:TOK], ACT.Copy, scale=vecs[:, 104 + c:105 + c]).then_inc(hsT_ready, 1)

            def mla(r):
                for c in range(12):
                    i, t = c // 3, c % 3
                    act.wait_ge(pl_full, c + 1)
                    n = 256 if i < 3 else ROPE
                    act.activation(pl[:, t, i * 256:i * 256 + n], ps[c % 4][:, 0:n], ACT.Copy).then_inc(pl_ready, 1)
                act.wait_ge(pl_ready, 12)
                for t in range(NT):
                    step(act.activation(knT[:, 0, :], pl[:, t, 0:QL], ACT.Square, accum_out=acol[:, t:t + 1]))
                    settle()
                for t in range(NT):
                    step(act.activation(knT[:, 0, 0:KVL], pl[:, t, QL:QL + KVL], ACT.Square, accum_out=acol[:, 3 + t:4 + t]))
                    settle()
                step(act.activation(acol[:, 6:9], acol[:, 0:3], ACT.Ln, scale=1.0 / QL, bias=eps[:, 0:1]))
                step(act.activation(acol[:, 9:12], acol[:, 3:6], ACT.Ln, scale=1.0 / KVL, bias=eps[:, 0:1]))
                settle()
                act.activation(acol[:, 12:18], acol[:, 6:12], ACT.Exp, scale=-0.5).then_inc(prs_ready, 1)
                for c in range(4):
                    act.wait_ge(ql_full, c + 1)
                    act.activation(qlT[:, c, :], ps[c][:, 0:TOK], ACT.Copy, scale=vecs[:, 112 + c:113 + c]).then_inc(ql_ready, 1)
                for c in range(2):
                    act.wait_ge(ck_full, c + 1)
                    act.activation(ckT[:, c, :], ps[4 + c][:, :], ACT.Copy).then_inc(ck_ready, 1)
                nq = 0
                for i in range(4):
                    for b in range(2):
                        act.wait_ge(qn_full, 2 * i + b + 1)
                        act.activation(qnT[:, 2 * i + b, :], ps[nq % 4][:, 0:TOK], ACT.Copy).then_inc(qn_ready, 1)
                        nq += 1
                    nq += 1
                for i in range(2):
                    for b in range(4):
                        h = 4 * i + b
                        act.wait_ge(kn_full, h + 1)
                        act.activation(knT[:, h, :], ps[4 + h % 2][:, :], ACT.Copy).then_inc(kn_ready, 1)
                for c in range(NT * AH):
                    h, t = c // NT, c % NT
                    n = CTX if t == 0 else KEYS - CTX
                    act.wait_ge(mx_ready, c + 1)
                    if c >= 2:
                        act.wait_ge(pt_full, c - 1)
                    act.activation(pr[:, c % 2, 0:n], ps[c % 3][:, 0:n], ACT.Exp, scale=SCALE, bias=acol[:, 20 + c % 4:21 + c % 4],
                                   accum_out=acol[:, 24 + c % 4:25 + c % 4]).then_inc(e_ready, 1)
                    if t == NT - 1:
                        act.wait_ge(pt_full, NT * (h + 1))
                        if h:
                            act.wait_ge(o_att, h)
                        act.activation(prT[:, 0:512], ps[3][:, :], ACT.Copy).then_inc(pt_ready, 1)
                        act.activation(prT[:, 512:896], ps[4][:, 0:384], ACT.Copy).then_inc(pt_ready, 1)

            def experts(L, n):
                act.wait_ge(rt_full, L + 1)
                act.activation(rt[:, 1, :], ps[5][:, 0:48], ACT.Exp, scale=-1.0).then_inc(rt_e, 1)
                with act.Fori(0, NE // UNROLL) as it:
                    for b in range(UNROLL):
                        g = NE * L + b
                        for f in range(2):
                            act.wait_ge(gu_full, it * (4 * UNROLL) + 4 * g + f + 1)
                            act.activation(sg[:, f, :], ps[f][:, 0:TOK], ACT.Exp, scale=-1.0).then_inc(sg_exp, 1)

            for L in range(LAYERS):
                kind = L % 3
                act.wait_ge(mod_ready, L + 1)
                norm(2 * L, mod[:, L, 0:8, :], hp_out if kind == 0 else h_out)
                if kind == 1:
                    mlstm(2 * L)
                elif kind == 2:
                    mla(2 * L)
                norm(2 * L + 1, mod[:, L, 24:32, :], h_out)
                experts(L, 2 * L + 1)
            norm(2 * LAYERS, None, None)
            for c in range(6):
                act.wait_ge(yt_full, c + 1)
                act.activation(yacc[:, :, :].rearrange("p k t -> p (k t)")[:, c * 512:(c + 1) * 512], ps[c % 4][:, :], ACT.Copy)\
                   .then_inc(yt_ready, 1)
            act.wait_ge(yt_ready, 6)
            y = yacc[:, :, :].rearrange("p k t -> p (k t)").rearrange("p (t d) -> p t d", t=NT)
            for t in range(NT):
                dst = O["y_prompt"][0] if t == 0 else O["y_sample"][0, (t - 1) * P:t * P]
                act.dma_start(dst, y[:, t, :]).then_inc(out_y, 16)
            act.wait_ge(out_y, 16 * NT)

        @block.vector
        def _(v):
            n_step = {"n": 0}

            def step(ins):
                ins.then_inc(vec_step, 1)
                n_step["n"] += 1

            def settle():
                v.wait_ge(vec_step, n_step["n"])

            v.wait_ge(vec_t, 1)
            v.tensor_copy(vecs[:, :], ps[6][:, 0:124]).then_inc(vec_cols, 1)
            for a in range(2):
                v.tensor_copy(b_ada[:, 96 * a:96 * (a + 1)], ps[6][:, 128 * (a + 1):128 * (a + 1) + 96]).then_inc(vec_cols, 1)
            for c in range(KC):
                v.wait_ge(xt_full, c + 1)
                v.tensor_copy(xT[:, c, :], ps[c % 4][:, 0:TOK]).then_inc(x_ready, 1)
            v.wait_ge(vec_cols, 3)
            v.wait_ge(cond_ready, 1)
            cc = vecs[:, 0:16].rearrange("p (c k) -> p k c", c=2)
            step(v.tensor_scalar(cond[:, :, :], cond[:, :, :], 1.0, None, ALU.add)); settle()
            step(v.reciprocal(cond[:, :, :], cond[:, :, :])); settle()
            v.tensor_tensor(cond[:, :, :], cond[:, :, :], cc, ALU.mult).then_inc(cond_ready, 1)

            def modulation(L):
                v.wait_ge(ada_unit, 24 * (L + 1))
                step(v.tensor_tensor(mod[:, L, :, :], ps[7][:, 0:96].rearrange("p (b c) -> p b c", c=2),
                                     b_ada[:, 48 * L:48 * (L + 1)].unsqueeze(2).to_broadcast([P, 48, 2]), ALU.add))
                settle()
                if L % 3 == 0:
                    j = L // 3
                    step(v.tensor_tensor(gpool[:, :, :], mod[:, L, 16:24, :],
                                         vecs[:, 88 + 8 * j:96 + 8 * j].unsqueeze(2).to_broadcast([P, KC, 2]), ALU.mult))
                for a, (m, o) in enumerate(((8, 16), (32, 48))):
                    g = vecs[:, o + 8 * L:o + 8 * L + 8].unsqueeze(2).to_broadcast([P, KC, 2])
                    ins = v.scalar_tensor_tensor(out=amp[:, a, :, :], in0=mod[:, L, m:m + 8, :], scalar=1.0, in1=g,
                                                 op0=ALU.add, op1=ALU.mult)
                ins.then_inc(mod_ready, 1)
                v.wait_ge(mod_ready, L + 1)

            def norm(n, gain):
                v.wait_ge(rstd_ready, n + 1)
                for k in range(KC):
                    for c in range(2):
                        a, b = SPAN[c]
                        g = gain[:, k, c:c + 1] if len(gain.shape) == 3 else gain[:, k:k + 1]
                        v.scalar_tensor_tensor(out=hT[:, k, a:b], in0=xT[:, k, a:b], scalar=g, in1=rstd[:, a:b],
                                               op0=ALU.mult, op1=ALU.mult).then_inc(h_scaled, 1)

            def residual(r, gate, src, wait):
                for c in range(KC):
                    if wait is not None:
                        v.wait_ge(y_full, wait + c + 1)
                    for q in range(2):
                        a, b = SPAN[q]
                        ins = v.scalar_tensor_tensor(out=xT[:, c, a:b], in0=src(c)[:, a:b], scalar=gate[:, c, q:q + 1],
                                                     in1=xT[:, c, a:b], op0=ALU.mult, op1=ALU.add)
                    ins.then_inc(x_ready, 1)

            def pool_mixer(r):
                v.wait_ge(h_ready, 16 * (r + 1))
                v.wait_ge(pads_set, 3 if r == 0 else 6)
                add = lambda o, a, b: v.tensor_tensor(o, a, b, ALU.add)
                step(add(ping[:, :, 1:HP], hp[:, :, 0:HP - 1], hp[:, :, 1:HP])); settle()
                step(add(pong[:, 2:8, 2:HP - 1], ping[:, 2:8, 1:HP - 2], ping[:, 2:8, 3:HP])); settle()
                step(add(ping[:, 4:8, 4:HP - 3], pong[:, 4:8, 2:HP - 5], pong[:, 4:8, 6:HP - 1])); settle()
                step(add(pong[:, 6:8, 8:HP - 7], ping[:, 6:8, 4:HP - 11], ping[:, 6:8, 12:HP - 3])); settle()
                v.wait_ge(inv_in, 16 if r == 0 else 32)
                for g in range(4):
                    src = (ping, pong)[g % 2]
                    for q in range(2):
                        a, b = SPAN[q]
                        o = HP_AT[q]
                        iv = inv[:, g, a:b].unsqueeze(1).to_broadcast([P, 2, b - a])
                        step(v.tensor_tensor(hT[:, 2 * g:2 * g + 2, a:b], src[:, 2 * g:2 * g + 2, o:o + b - a], iv, ALU.mult))
                    settle()
                    for q in range(2):
                        a, b = SPAN[q]
                        o = HP_AT[q]
                        ins = v.tensor_tensor(hT[:, 2 * g:2 * g + 2, a:b], hT[:, 2 * g:2 * g + 2, a:b],
                                              hp[:, 2 * g:2 * g + 2, o:o + b - a], ALU.subtract)
                    ins.then_inc(pooled, 1)

            def mlstm(r):
                v.tensor_copy(cx[:, :, :, DV:VX].rearrange("p d h o -> p (d h o)"), vecs[:, 116:124]).then_inc(state_set, 1)
                v.wait_ge(gate_full, 1)
                v.tensor_tensor(g_tok, ps[4][:, 0:48].rearrange("p (t g) -> p t g", t=NT),
                                b_gt[:, :].unsqueeze(1).to_broadcast([P, NT, 16]), ALU.add).then_inc(gate_tok, 1)
                v.wait_ge(grow_full, 1)
                v.wait_ge(softplus, 1)
                for d in range(2):
                    step(v.scalar_tensor_tensor(out=rI[:, d, :], in0=ps[2 * d + 1][0:MH, 0:TOK], scalar=0.0, in1=rI[:, d, :],
                                                op0=ALU.min, op1=ALU.subtract))
                settle()

                def seq(row, d, q):
                    a, b = SPAN[q]
                    s = row[:, d, a:b]
                    return s if d == 0 else s[:, ::-1]

                for d in range(2):
                    for q in range(2):
                        n = SPAN[q][1] - SPAN[q][0]
                        step(v.tensor_tensor_scan(seq(rB, d, q), ones[0:MH, 0:1].to_broadcast([MH, n]), seq(rI, d, q),
                                                  0.0, ALU.mult, ALU.add))
                settle()
                for d in range(2):
                    step(v.tensor_tensor(rA[:, d, :], ps[2 * d][0:MH, 0:TOK], rB[:, d, :], ALU.subtract))
                settle()
                for d in range(2):
                    for q in range(2):
                        step(v.tensor_tensor_scan(seq(rM, d, q), seq(rA, d, q), seq(rA, d, q),
                                                  0.0 if q == 0 else m0[:, d:d + 1], ALU.max, ALU.max))
                settle()
                step(v.tensor_tensor(rE[:, :, :], rM[:, :, :], rB, ALU.add))
                settle()
                v.tensor_copy(rS[:, :, 0:CTX], rM[:, :, 0:CTX])
                for d in range(2):
                    ins = v.tensor_scalar(rS[:, d, CTX:TOK], rM[:, d, CTX:TOK], m0[:, d:d + 1], None, ALU.subtract)
                ins.then_inc(rows_done, 1)
                v.wait_ge(rowc_full, 1)
                v.tensor_copy(rowc.rearrange("p d k t h -> p (d k t h)"), ps[4][:, 64:136]).then_inc(rowc_set, 1)
                for i in range(MH):
                    for t in range(NT):
                        v.wait_ge(l_ready, NT * i + t + 1)
                        o = og[:, t, i, :]
                        step(v.tensor_scalar(o, o, 1.0, None, ALU.add)); settle()
                        v.reciprocal(o, o).then_inc(o_ready, 1)
                npj = 0
                nl = n_hs = 0
                v.wait_ge(tables_in, 32)
                for h in range(MH):
                    for d in range(2):
                        v.wait_ge(mbc_full, 2 * h + d + 1)
                        if h:
                            v.wait_ge(w_ready, 2 * h)
                        v.tensor_tensor(mm_[:, d, :].rearrange("p (b t) -> p b t", b=NT),
                                        ps[2 + d][:, 0:TOK].rearrange("p (b t) -> p b t", b=NT),
                                        mask[:, d, :].unsqueeze(1).to_broadcast([P, NT, P]), ALU.add).then_inc(mm_ready, 1)
                    v.wait_ge(s_full, h + 1)
                    if h:
                        v.wait_ge(p_full, npj)
                    for d in range(2):
                        v.wait_ge(w_ready, 2 * h + d + 1)
                        col = wgt[:, d, P - 1:P] if d == 0 else wgt[:, d, 0:1]
                        v.tensor_scalar(kkb[:, d, :], ps[1][:, P:2 * P], col, None, ALU.mult).then_inc(kk_ready, 1)
                        if d == 0:
                            v.tensor_tensor(aT[:, 0, :], wgt[:, 0, :], ps[0][:, :], ALU.mult).then_inc(at_ready, 1)
                        else:
                            v.tensor_tensor(aT[:, 1, 0:TOK], wgt[:, 1, 0:TOK], ps[0][:, 0:TOK], ALU.mult).then_inc(at_ready, 1)
                            v.tensor_tensor(aT[:, 1, TOK:512], wgt[:, 1, TOK:512], ps[1][:, 0:P], ALU.mult).then_inc(at_ready, 1)
                    for d in range(2):
                        npj += 1
                        v.wait_ge(p_full, npj)
                        if h or d:
                            v.wait_ge(out_c, 16 * (2 * h + d))
                        v.tensor_copy(c_st[:, :], ps[4 + (npj - 1) % 3][:, 0:DV]).then_inc(c_copied, 1)
                        v.tensor_copy(nout[:, MH * d + h:MH * d + h + 1], ps[4 + (npj - 1) % 3][:, DV:VX]).then_inc(p_used, 1)
                        for t in range(NT):
                            npj += 1
                            v.wait_ge(p_full, npj)
                            p2 = ps[4 + (npj - 1) % 3][:, 0:VX]
                            if n_hs:
                                v.wait_ge(ss_ready, n_hs)
                            if t == 0:
                                v.tensor_copy(nd, p2).then_inc(p_used, 1)
                            else:
                                npj += 1
                                nl += 1
                                v.wait_ge(p1_ready, nl)
                                v.tensor_tensor(nd, p1s, p2, ALU.add).then_inc(p_used, 2)
                            v.wait_ge(p_used, npj)
                            en = rowc[:, d, 2, t, h:h + 1]
                            den = nd[:, DV:VX]
                            step(v.scalar_tensor_tensor(out=dcol[:, 2:3], in0=den, scalar=-1.0, in1=den,
                                                        op0=ALU.mult, op1=ALU.max)); settle()
                            step(v.tensor_tensor(dcol[:, 0:1], dcol[:, 2:3], en, ALU.max)); settle()
                            step(v.reciprocal(dcol[:, 1:2], dcol[:, 0:1])); settle()
                            o = hs[:, t, h, :]
                            if d == 0:
                                step(v.tensor_scalar(o, nd[:, 0:DV], dcol[:, 1:2], None, ALU.mult)); settle()
                            else:
                                v.scalar_tensor_tensor(out=o, in0=nd[:, 0:DV], scalar=dcol[:, 1:2], in1=o,
                                                       op0=ALU.mult, op1=ALU.add).then_inc(ss_ready, 1)
                                n_hs += 1
                v.wait_ge(nt_full, 1)
                v.tensor_copy(n_t[0:8, :], ps[2][0:8, 0:P]).then_inc(n_copied, 1)
                v.wait_ge(hrs_ready, 1)
                v.wait_ge(o_ready, 12)
                for h in range(MH):
                    for t in range(NT):
                        v.scalar_tensor_tensor(out=hs[:, t, h, :], in0=hs[:, t, h, :], scalar=hrs[:, NT * h + t:NT * h + t + 1],
                                               in1=og[:, t, h, :], op0=ALU.mult, op1=ALU.mult).then_inc(hn_ready, 1)

            def mla(r):
                v.wait_ge(prs_ready, 1)
                for t in range(NT):
                    v.tensor_scalar(pl[:, t, 0:QL], pl[:, t, 0:QL], acol[:, 12 + t:13 + t], None, ALU.mult).then_inc(pn_ready, 1)
                for t in range(NT):
                    v.scalar_tensor_tensor(out=pl[:, t, QL:QL + KVL], in0=pl[:, t, QL:QL + KVL], scalar=acol[:, 15 + t:16 + t],
                                           in1=g_kv[:, :], op0=ALU.mult, op1=ALU.mult).then_inc(pn_ready, 1)
                v.wait_ge(pl_ready, 12)
                for s in (0, 2, 3):
                    t = max(s - 1, 0)
                    for half in range(2):
                        ins = v.tensor_copy(kp2[:, s, half * ROPE:(half + 1) * ROPE], pl[:, t, QL + KVL:])
                ins.then_inc(kp_dup, 1)
                v.wait_ge(kp_full, 1)
                v.tensor_copy(kpT, ps[6][:, :]).then_inc(kp_ready, 1)
                v.wait_ge(kp_ready, 1)

                def rope(i, x):
                    v.wait_ge(rot_full, i + 1)
                    step(v.tensor_tensor(t_rot, ps[6][:, 0:LAT], trig[:, 1, :], ALU.mult))
                    step(v.tensor_tensor(t_cos, x, trig[:, 0, :], ALU.mult))
                    settle()
                    v.tensor_tensor(x, t_rot, t_cos, ALU.add).then_inc(rope_ready, 1)
                    v.wait_ge(rope_ready, i + 1)

                v.wait_ge(out_kv, 32)
                v.wait_ge(ck_full, 2)
                v.wait_ge(ql_full, 4)
                rope(0, kpT[:, KEYS - LAT:KEYS])
                for i in range(4):
                    v.wait_ge(qp_full, i + 1)
                    v.tensor_copy(qpT[:, i, :], ps[(3 * i + 2) % 4][:, 0:TOK]).then_inc(qp_raw, 1)
                v.wait_ge(qp_raw, 4)
                for i in range(4):
                    rope(i + 1, qpT[:, i, CTX:TOK])
                for c in range(8):
                    v.wait_ge(vt_full, c + 1)
                    i, s = c // 4, c % 4
                    v.tensor_copy(vt[:, s, 4 * i:4 * i + 4, :], ps[c % 4][:, :].rearrange("p (h n) -> p h n", h=4)).then_inc(vt_ready, 1)

                def peak(c):
                    n = CTX if c % NT == 0 else KEYS - CTX
                    v.wait_ge(sc_full, c + 1)
                    if c >= 4:
                        v.wait_ge(e_ready, c - 3)
                    step(v.tensor_reduce(acol[:, 28:29], ps[c % 3][:, 0:n], AX.X, ALU.max)); settle()
                    v.tensor_scalar(acol[:, 20 + c % 4:21 + c % 4], acol[:, 28:29], -SCALE, None, ALU.mult).then_inc(mx_ready, 1)
                    v.wait_ge(mx_ready, c + 1)

                peak(0)
                for c in range(NT * AH):
                    if c + 1 < NT * AH and (c + 1) % NT:
                        peak(c + 1)
                    n = CTX if c % NT == 0 else KEYS - CTX
                    v.wait_ge(e_ready, c + 1)
                    step(v.reciprocal(acol[:, 30 + c % 2:31 + c % 2], acol[:, 24 + c % 4:25 + c % 4])); settle()
                    v.tensor_scalar(pr[:, c % 2, 0:n], pr[:, c % 2, 0:n], acol[:, 30 + c % 2:31 + c % 2], None, ALU.mult)\
                     .then_inc(p_ready, 1)
                    if c % NT == NT - 1:
                        h = c // NT
                        if c + 1 < NT * AH:
                            peak(c + 1)
                        v.wait_ge(o_att, h + 1)
                        v.tensor_copy(hT[:, h, :], ps[5 + h % 2][:, 0:TOK]).then_inc(oT_ready, 1)

            def best_of_four(val, n, cnt, cmp):
                step(v.memset(cnt, 0.0))
                settle()
                for i in range(4):
                    for q in range(i + 1, 4):
                        step(v.tensor_tensor(cmp, val[:, :, i], val[:, :, q], ALU.is_ge)); settle()
                        step(v.tensor_tensor(cnt[:, :, q], cnt[:, :, q], cmp, ALU.add))
                        step(v.scalar_tensor_tensor(out=cnt[:, :, i], in0=cnt[:, :, i], scalar=1.0, in1=cmp,
                                                    op0=ALU.add, op1=ALU.subtract))
                        settle()

            def experts(L, n):
                v.wait_ge(rt_e, L + 1)
                sc = rt[:, 1, :]
                step(v.tensor_scalar(sc, sc, 1.0, None, ALU.add)); settle()
                step(v.reciprocal(sc, sc)); settle()
                se = rt[:, 2, :]
                step(v.tensor_tensor(se.rearrange("p (t e) -> p t e", t=NT), sc.rearrange("p (t e) -> p t e", t=NT),
                                     b_rt[:, :].unsqueeze(1).to_broadcast([P, NT, NE]), ALU.add)); settle()
                cnt = rt[:, 3, :].rearrange("p (g e) -> p g e", e=4)
                best_of_four(se.rearrange("p (g e) -> p g e", e=4), 12, cnt, rt[:, 4, 0:12])
                pick = rt[:, 5, :]
                step(v.tensor_scalar(pick, rt[:, 3, :], 2.0, None, ALU.is_lt)); settle()
                top = rt[:, 6, :]
                step(v.tensor_tensor(top, pick, se, ALU.mult)); settle()
                gs = rt[:, 7, 0:12]
                step(v.tensor_reduce(gs, top.rearrange("p (g e) -> p g e", e=4), AX.X, ALU.add)); settle()
                gc = rt[:, 8, 0:12].rearrange("p (t g) -> p t g", g=4)
                best_of_four(gs.rearrange("p (t g) -> p t g", g=4), 3, gc, rt[:, 4, 0:3])
                gb = rt[:, 9, 0:12]
                step(v.tensor_scalar(gb, rt[:, 8, 0:12], 0.0, None, ALU.is_equal)); settle()
                step(v.tensor_tensor(pick.rearrange("p (g e) -> p g e", e=4), pick.rearrange("p (g e) -> p g e", e=4),
                                     gb.unsqueeze(2).to_broadcast([P, 12, 4]), ALU.mult)); settle()
                step(v.tensor_tensor(pick, pick, sc, ALU.mult)); settle()
                sm = rt[:, 10, 0:3]
                step(v.tensor_reduce(sm, pick.rearrange("p (t e) -> p t e", t=NT), AX.X, ALU.add)); settle()
                step(v.reciprocal(sm, sm)); settle()
                v.tensor_tensor(rt[:, 0, :].rearrange("p (t e) -> p t e", t=NT), pick.rearrange("p (t e) -> p t e", t=NT),
                                sm.unsqueeze(2).to_broadcast([P, NT, NE]), ALU.mult).then_inc(comb_tok, 1)
                v.wait_ge(combT_full, L + 1)
                v.tensor_copy(combT[0:NE, :], ps[5][0:NE, 64:64 + TOK]).then_inc(combT_ready, 1)
                step(v.memset(yacc[:, :, :], 0.0)); settle()
                n0 = n_step["n"]
                per = 8
                with v.Fori(0, NE // UNROLL) as it:
                    s = 0
                    for b in range(UNROLL):
                        g = NE * L + b
                        for f in range(2):
                            def fence(s):
                                v.wait_ge(vec_step, it * (UNROLL * 2 * 4) + n0 + s)
                            v.wait_ge(sg_exp, it * (2 * UNROLL) + 2 * g + f + 1)
                            a = sg[:, f, :]
                            v.tensor_scalar(a, a, 1.0, None, ALU.add).then_inc(vec_step, 1); s += 1; fence(s)
                            v.reciprocal(a, a).then_inc(vec_step, 1); s += 1; fence(s)
                            v.tensor_tensor(a, a, ps[f][:, 0:TOK], ALU.mult).then_inc(vec_step, 1); s += 1; fence(s)
                            v.wait_ge(gu_full, it * (4 * UNROLL) + 4 * g + 3 + f)
                            v.tensor_tensor(a, a, ps[2 + f][:, 0:TOK], ALU.mult).then_inc(vec_step, 1); s += 1; fence(s)
                            v.wait_ge(cb_full, it * UNROLL + g + 1)
                            v.tensor_tensor(hid[:, f, :], a, ps[4][:, 0:TOK], ALU.mult).then_inc(hid_ready, 1)
                        for c in range(KC):
                            v.wait_ge(yp_full, it * (8 * UNROLL) + 8 * g + c + 1)
                            v.tensor_tensor(yacc[:, c, :], yacc[:, c, :], ps[5 + c % 2][:, 0:TOK], ALU.add).then_inc(yp_used, 1)
                n_step["n"] = n0 + NE * 2 * 4
                v.wait_ge(yp_used, 8 * NE * (L + 1))

            modulation(0)
            for L in range(LAYERS):
                kind = L % 3
                norm(2 * L, amp[:, 0, :, :])
                if kind == 0:
                    pool_mixer(2 * L)
                elif kind == 1:
                    mlstm(2 * L)
                else:
                    mla(2 * L)
                residual(2 * L, gpool if kind == 0 else mod[:, L, 16:24, :], lambda c: ps[c % 4], 8 * L)
                norm(2 * L + 1, amp[:, 1, :, :])
                experts(L, 2 * L + 1)
                residual(2 * L + 1, mod[:, L, 40:48, :], lambda c: yacc[:, c, :], None)
                if L + 1 < LAYERS:
                    modulation(L + 1)
            norm(2 * LAYERS, vecs[:, 80:88])

        @block.gpsimd
        def _(g):
            g.memset(ones[:, :], 1.0).then_inc(pool_set, 1)
            g.memset(mean_ones[:, :], 1.0 / D).then_inc(pool_set, 1)
            g.memset(eps[:, :], EPS).then_inc(pool_set, 1)

            def pooling_tables(n):
                for a, b in ((0, PAD), (PAD + CTX, 2 * PAD + CTX), (HP - PAD, HP)):
                    g.memset(hp[:, :, a:b], 0.0).then_inc(pads_set, 1)
                g.dma_start(inv[:, :, :], A["k_inv"].partition_broadcast(P)).then_inc(inv_in, 16)

            g.wait_ge(vec_t, 1)
            g.wait_ge(xt_full, KC)
            pooling_tables(0)
            def combine_rows(L):
                g.wait_ge(combT_ready, L + 1)
                g.dma_start(comb_row[0:1, :, :], combT[0:NE, :]).then_inc(comb_rows, 16)

            combine_rows(0)
            g.wait_ge(x_ready, 24)
            g.memset(vx[:, :, :, DV:VX], 1.0).then_inc(vx_ones, 1)
            g.dma_start(mask[:, :, :], A["k_mask"]).then_inc(tables_in, 16)
            g.dma_start(sel, A["k_sel"]).then_inc(tables_in, 16)
            for d in range(2):
                g.dma_start(cx[:, d, :, 0:DV], A["state_mlstm_C"][0, 0, d].rearrange("h k v -> k h v")).then_inc(state_in, 16)
            with nc.allow_non_contiguous_dma(reason="eight floats"):
                g.wait_ge(rows_done, 1)
                g.dma_start(O["new_m"][0, 0, 0].rearrange("(h o) -> h o", o=1), rE[:, 0, CTX - 1:CTX]).then_inc(out_m, 16)
                g.dma_start(O["new_m"][0, 0, 1].rearrange("(h o) -> h o", o=1), rE[:, 1, 0:1]).then_inc(out_m, 16)
            for h in range(MH):
                for d in range(2):
                    g.wait_ge(c_copied, 2 * h + d + 1)
                    g.dma_start(O["new_C"][0, 0, d, h], c_st).then_inc(out_c, 16)
            g.wait_ge(n_copied, 1)
            g.dma_start(O["new_n"].rearrange("b l d h k -> (b l d h) k"), n_t[0:8, :]).then_inc(out_n, 16)
            g.wait_ge(out_m, 32)
            g.wait_ge(out_c, 16 * 8)
            g.wait_ge(out_n, 16)
            combine_rows(1)
            g.wait_ge(pl_full, 12)
            g.dma_start(cache, A["cache_mla_ckv"][0, 0]).then_inc(cache_in, 16)
            for half in range(2):
                g.dma_start(kp2[:, 1, half * ROPE:(half + 1) * ROPE], A["cache_mla_kpe"][0, 0]).then_inc(cache_in, 16)
            g.wait_ge(pl_ready, 12)
            g.dma_start(O["new_kpe"][0, 0], pl[:, 0, QL + KVL:]).then_inc(out_kv, 16)
            g.wait_ge(pn_ready, 4)
            g.dma_start(O["new_ckv"][0, 0], pl[:, 0, QL:QL + KVL]).then_inc(out_kv, 16)
            g.wait_ge(out_kv, 32)
            combine_rows(2)
            g.wait_ge(x_ready, 56)
            pooling_tables(1)
            g.wait_ge(inv_in, 32)
            combine_rows(3)
            g.wait_ge(comb_rows, 64)


INPUTS = ["x_prompt", "x_sample", "state_mlstm_C", "state_mlstm_n", "state_mlstm_m", "cache_mla_ckv", "cache_mla_kpe",
          "c", "c_ctx", "w_ada", "b_ada", "norm_mix", "norm_ffn", "norm_final", "w_pool", "pool_scale", "w_mlstm_in",
          "b_mlstm_gate", "mlstm_head_g", "w_mlstm_out", "w_mla_in", "mla_q_g", "mla_kv_g", "w_mla_qb", "w_mla_kvb",
          "w_mla_out", "w_router", "b_router", "w_exp_gate", "w_exp_up", "w_exp_down"]
OUTPUTS = [("y_prompt", (1, CTX, D)), ("y_sample", (1, LAT, D)), ("new_C", (1, 1, 2, MH, DK, DV)),
           ("new_n", (1, 1, 2, MH, DK)), ("new_m", (1, 1, 2, MH)), ("new_ckv", (1, 1, CTX, KVL)),
           ("new_kpe", (1, 1, CTX, ROPE))]


def kernel(**inputs):
    import concourse.bacc as bacc
    from concourse.bass_utils import run_bass_kernel_spmd

    nc = bacc.Bacc("TRN2", target_bir_lowering=False, num_devices=1)
    arrays = {name: np.ascontiguousarray(inputs[name]) for name in INPUTS}
    arrays.update(constants())
    A = {name: nc.dram_tensor("in_" + name, a.shape, mybir.dt.from_np(a.dtype), kind="ExternalInput").ap()
         for name, a in arrays.items()}
    O = {name: nc.dram_tensor("out_" + name, shape, F32, kind="ExternalOutput").ap() for name, shape in OUTPUTS}
    build(nc, A, O)
    r = run_bass_kernel_spmd(nc, [{"in_" + k: a for k, a in arrays.items()}], core_ids=[0])
    return tuple(r.results[0]["out_" + name] for name, _ in OUTPUTS)
```

```python
from contextlib import ExitStack

import numpy as np

import concourse.bass as bass
from concourse import mybir

F32 = mybir.dt.float32
U32 = mybir.dt.uint32
ALU = mybir.AluOpType
ACT = mybir.ActivationFunctionType
AX = mybir.AxisListType

P = 128
D = 1024
KC = D // P
CTX, LAT = 128, 256
TOK = CTX + LAT
NT = TOK // P
SPAN = [(0, CTX), (CTX, TOK)]
LAYERS = 4
EPS = 1e-6
WINDOWS = (2, 4, 8, 16)
PAD = 8
HP = PAD + CTX + PAD + LAT + PAD
HP_AT = [PAD, PAD + CTX + PAD]
MH, DK, DV = 4, 128, 256
AH, NOPE, ROPE, VD = 8, 128, 64, 128
QL, KVL = 512, 256
PAST = 128
KEYS = CTX + PAST + LAT
SCALE = float((NOPE + ROPE) ** -0.5)
GRID_W = 64
NE, FE = 16, 256
UNROLL = 4
SLOTS = P
CAP = SLOTS
NOWHERE = 5000.0
UNIT = 2048
RING = 3 * UNROLL


def constants():
    s = np.arange(P)
    ident = np.eye(P, dtype=np.float32)
    mask = np.zeros((P, 2, P), np.float32)
    mask[:, 0] = np.where(s[:, None] > s[None, :], 1e30, 0.0)
    mask[:, 1] = np.where(s[:, None] < s[None, :], 1e30, 0.0)
    inv = np.zeros((len(WINDOWS), TOK), np.float32)
    for g, w in enumerate(WINDOWS):
        for a, b in SPAN:
            t = np.arange(b - a)
            inv[g, a:b] = 1.0 / (np.clip(t + w // 2, 0, b - a) - np.clip(t - w // 2, 0, b - a))
    half = ROPE // 4
    freq = np.power(np.float32(10000.0), -np.arange(half, dtype=np.float32) / half).astype(np.float32)
    pos = [np.arange(LAT) // GRID_W, np.arange(LAT) % GRID_W]
    ang = np.concatenate([np.tile(p[None, :].astype(np.float32) * freq[:, None], (2, 1)) for p in pos])
    trig = np.stack([np.tile(np.cos(ang), (2, 1)), np.tile(np.sin(ang), (2, 1))], 1).astype(np.float32)
    rot = np.zeros((P, P), np.float32)
    for m in range(P):
        if m % 32 < half:
            rot[m + half, m] = -1.0
        else:
            rot[m - half, m] = 1.0
    sel = np.zeros((MH, MH, P), np.float32)
    for h in range(MH):
        sel[h, h] = 1.0
    tri = (s[:, None] < s[None, :]).astype(np.float32)
    base = (np.arange(NE) * SLOTS + 1).astype(np.float32)
    return {"k_tri": tri, "k_base": base, "k_ident": ident, "k_mask": mask, "k_inv": inv, "k_trig": trig, "k_rot": rot, "k_sel": sel}


def build(nc, A, O, Xg, Yg):
    ctx = ExitStack()
    with ctx:
        def sb(name, shape):
            return ctx.enter_context(nc.sbuf_tensor("sb_" + name, shape, F32))

        def sem(name):
            return ctx.enter_context(nc.semaphore(name))

        ps = [ctx.enter_context(nc.psum_tensor(f"bank{i}", [P, 512], F32)) for i in range(8)]

        xT = sb("xT", [P, KC, TOK])
        hT = sb("hT", [P, KC, TOK])
        scratch = sb("scratch", [P, KC * HP])
        ring = sb("ring", [P, RING, UNIT])
        ident = sb("ident", [P, P])
        mean_ones = sb("mean_ones", [P, P])
        ones = sb("ones", [P, P])
        trig = sb("trig", [P, 2, LAT])
        rot = sb("rot", [P, P])
        w_rt = sb("w_rt", [P, KC, NE])
        w_gt = sb("w_gt", [P, KC, 16])
        w_kp = sb("w_kp", [P, KC, ROPE])
        b_rt = sb("b_rt", [P, NE])
        b_gt = sb("b_gt", [P, 16])
        g_kv = sb("g_kv", [P, KVL])
        vecs = sb("vecs", [P, 124])
        b_ada = sb("b_ada", [P, LAYERS * 48])
        cond = sb("cond", [P, KC, 2])
        mod = sb("mod", [P, LAYERS, 48, 2])
        mrow = sb("mrow", [P, 512])
        amp = sb("amp", [P, 2, KC, 2])
        gpool = sb("gpool", [P, KC, 2])
        rstd = sb("rstd", [P, TOK])
        m0 = sb("m0", [MH, 2])
        eps = sb("eps", [P, 1])
        tri = sb("tri", [P, P])
        base = sb("base", [P, NE])
        slots = ctx.enter_context(nc.sbuf_tensor("sb_slots", [P, 2 * NT], U32))
        spill = ctx.enter_context(nc.sbuf_tensor("sb_spill", [P, 1], U32))
        acol = sb("acol", [P, 64])
        arena = sb("arena", [P, 15104])

        sq = scratch[:, 0:KC * TOK].rearrange("p (k t) -> p k t", k=KC)

        def view(off, *dims):
            n = int(np.prod(dims))
            assert off + n <= 15104, (off, dims)
            v = arena[:, off:off + n]
            if len(dims) == 2:
                v = v.rearrange("p (a b) -> p a b", a=dims[0])
            elif len(dims) == 3:
                v = v.rearrange("p (a b c) -> p a b c", a=dims[0], b=dims[1])
            elif len(dims) == 4:
                v = v.rearrange("p (a b c d) -> p a b c d", a=dims[0], b=dims[1], c=dims[2])
            return v

        x_in = view(0, NT, D)
        rows_in = view(3072, 3, P)
        hp = view(0, KC, HP)
        pong = view(KC * HP, KC, HP)
        inv = view(2 * KC * HP, 4, TOK)
        ping = scratch[:, :].rearrange("p (k t) -> p k t", k=KC)
        qT = view(0, MH, TOK)
        kT = view(1536, MH, TOK)
        VX = DV + 1
        vx = view(3072, NT, MH, VX)
        hs = view(3072 + 3084, NT, MH, DV)
        cx = view(9228, 2, MH, VX)
        hflat = hT[:, :, :].rearrange("p k t -> p (k t)")
        wgt = hflat[:, 0:1024].rearrange("p (d n) -> p d n", d=2)
        aT = hflat[:, 1024:2048].rearrange("p (d n) -> p d n", d=2)
        mm_ = hflat[:, 2048:2816].rearrange("p (d n) -> p d n", d=2)
        nd = view(11284, VX)
        p1s = view(11541, VX)
        c_st = view(11798, DV)
        mask = view(12054, 2, P)
        sel = view(12310, MH, P)[0:MH]
        kkb = view(12822, 2, P)
        n_t = view(13078, P)
        rM = view(13206, 2, TOK)[0:MH]
        rE = view(13974, 2, TOK)[0:MH]
        small = view(14742, 160)
        g_tok = small[:, 0:48].rearrange("p (t g) -> p t g", t=NT)
        rowc = small[:, 48:120].rearrange("p (d k t h) -> p d k t h", d=2, k=3, t=NT)
        ssq = small[:, 120:132]
        hrs = small[:, 132:144]
        dcol = small[:, 144:148]
        nout = small[:, 148:156]
        og = scratch[:, 0:NT * D].rearrange("p (t h d) -> p t h d", t=NT, h=MH)
        grow = view(3072 + 3084, 8, TOK)
        rI = grow[0:MH, 0:2, :]
        rB = grow[0:MH, 2:4, :]
        rA = grow[0:MH, 4:6, :]
        rS = grow[0:MH, 6:8, :]

        pl = view(0, NT, QL + KVL + ROPE)
        qlT = view(2496, QL // P, TOK)
        qpT = view(4032, AH // 2, TOK)
        knT = view(5568, AH, KEYS)
        vt = view(9664, KEYS // P, AH, VD)
        ckT = view(13760, KVL // P, KEYS)
        kpT = w_kp[:, :, :].rearrange("p k r -> p (k r)")
        qnT = scratch[:, 0:AH * TOK].rearrange("p (h t) -> p h t", h=AH)
        pr = view(0, 2, TOK)
        prT = view(768, 896)
        t_rot = view(1664, LAT)
        t_cos = view(1920, LAT)
        cache = hT[:, 0, 0:KVL]
        kp2 = hT[:, 1:3, :].rearrange("p a t -> p (a t)")[:, 0:512].rearrange("p (t r) -> p t r", t=4)

        htok = view(0, NT, D)
        yg = view(0, NT, 2, D)
        xg = view(3072, 2, D)
        xgT = view(5120, 2, KC, P)
        ysb = view(7168, 2, D)
        sil = view(9216, 2, FE)
        hid = view(9728, 2, FE)
        hidT = view(10240, 2, P)
        rt = view(11136, 40, NT * NE)
        zeros = view(8192, D)
        yacc = view(0, KC, TOK)
        hidF = view(3072, 2, TOK)
        sg = view(3840, 2, TOK)
        combT = view(4608, TOK)
        comb_row = view(4992, NE, TOK)
        wF = view(13056, UNIT)

        const_in = sem("const_in"); x_loaded = sem("x_loaded"); rows_loaded = sem("rows_loaded")
        pool_set = sem("pool_set"); vec_t = sem("vec_t"); vec_cols = sem("vec_cols")
        xt_full = sem("xt_full"); x_ready = sem("x_ready"); cond_ready = sem("cond_ready")
        slot_in = [sem(f"slot_in{i}") for i in range(RING)]
        ada_full = sem("ada_full"); ident_in = sem("ident_in"); ada_unit = sem("ada_unit"); mrow_ready = sem("mrow_ready"); mod_added = sem("mod_added"); bank7_set = sem("bank7_set")
        sq_ready = sem("sq_ready"); ms_full = sem("ms_full"); rstd_ready = sem("rstd_ready")
        h_scaled = sem("h_scaled"); h_ready = sem("h_ready")
        act_step = sem("act_step"); vec_step = sem("vec_step")
        y_full = sem("y_full")
        inv_in = sem("inv_in"); pads_set = sem("pads_set"); pooled = sem("pooled")
        gate_full = sem("gate_full"); gate_tok = sem("gate_tok"); grow_full = sem("grow_full")
        rows_done = sem("rows_done"); rowc_full = sem("rowc_full"); rowc_ready = sem("rowc_ready")
        qk_full = sem("qk_full"); qk_ready = sem("qk_ready"); v_full = sem("v_full"); v_ready = sem("v_ready")
        o_full = sem("o_full"); o_ready = sem("o_ready"); state_in = sem("state_in"); state_set = sem("state_set")
        s_full = sem("s_full"); mbc_full = sem("mbc_full"); mm_ready = sem("mm_ready")
        w_ready = sem("w_ready"); at_ready = sem("at_ready"); kk_ready = sem("kk_ready")
        c_copied = sem("c_copied"); p_full = sem("p_full"); p1_ready = sem("p1_ready")
        p_used = sem("p_used"); softplus = sem("softplus")
        ss_ready = sem("ss_ready"); hrs_ready = sem("hrs_ready"); hn_ready = sem("hn_ready")
        hsT_full = sem("hsT_full"); hsT_ready = sem("hsT_ready"); nt_full = sem("nt_full"); n_copied = sem("n_copied"); rowc_set = sem("rowc_set"); vx_ones = sem("vx_ones"); tables_in = sem("tables_in")
        out_c = sem("out_c"); out_n = sem("out_n"); out_m = sem("out_m"); l_ready = sem("l_ready")
        pl_full = sem("pl_full"); pl_ready = sem("pl_ready"); pn_ready = sem("pn_ready"); prs_ready = sem("prs_ready")
        cache_in = sem("cache_in"); kp_dup = sem("kp_dup"); ql_full = sem("ql_full"); ql_ready = sem("ql_ready")
        ck_full = sem("ck_full"); ck_ready = sem("ck_ready"); kp_full = sem("kp_full"); kp_ready = sem("kp_ready")
        rot_full = sem("rot_full"); rope_ready = sem("rope_ready"); qn_full = sem("qn_full"); qn_ready = sem("qn_ready")
        qp_full = sem("qp_full"); qp_raw = sem("qp_raw"); kn_full = sem("kn_full"); kn_ready = sem("kn_ready")
        vt_full = sem("vt_full"); vt_ready = sem("vt_ready"); sc_full = sem("sc_full"); mx_ready = sem("mx_ready")
        e_ready = sem("e_ready"); p_ready = sem("p_ready"); pt_full = sem("pt_full"); pt_ready = sem("pt_ready")
        o_att = sem("o_att"); oT_ready = sem("oT_ready"); out_kv = sem("out_kv")
        rt_full = sem("rt_full"); rt_e = sem("rt_e"); ht_full = sem("ht_full"); ht_ready = sem("ht_ready")
        mask_ready = sem("mask_ready"); pos_full = sem("pos_full"); slots_ready = sem("slots_ready")
        zeros_set = sem("zeros_set"); zeroed = sem("zeroed"); scattered = sem("scattered")
        xg_in = [sem(f"xg_in{i}") for i in range(2)]; xt_full2 = sem("xgT_full"); xa_ready = sem("xa_ready"); xb_ready = sem("xb_ready")
        gu_full = sem("gu_full"); sil_ready = sem("sil_ready"); hid_ready = sem("hid_ready"); hidT_full = sem("hidT_full")
        hidT_ready = sem("hidT_ready"); yp_full = sem("yp_full"); ya_ready = sem("ya_ready"); yb_ready = sem("yb_ready")
        y_stored = [sem(f"y_stored{i}") for i in range(2)]; yg_in = [sem(f"yg_in{i}") for i in range(NT)]
        yw_ready = sem("yw_ready"); ys_ready = sem("ys_ready"); yc_full = sem("yc_full")
        f_comb = sem("f_comb"); f_combT = sem("f_combT"); f_combT_ready = sem("f_combT_ready"); f_rows = sem("f_rows")
        f_w = sem("f_w"); f_gu = sem("f_gu"); f_cb = sem("f_cb"); f_sg = sem("f_sg"); f_hid = sem("f_hid")
        f_y = sem("f_y"); f_yused = sem("f_yused"); f_zero = sem("f_zero"); f_step = sem("f_step"); f_free = sem("f_free"); spill_done = sem("spill_done")
        yt_full = sem("yt_full"); yt_ready = sem("yt_ready"); out_y = sem("out_y")

        NCONST = 11

        units = []

        def slot(u):
            return ring[:, u % RING, :]

        def add(src, cols, release):
            units.append((src, cols, release))

        def ada_units(*halves):
            for half in halves:
                L, s = half // 6, half % 6
                for q in range(4):
                    b = 4 * (s // 2) + q
                    add((A["w_ada"][L, (s % 2) * 512:(s % 2 + 1) * 512, b * 512:(b + 1) * 512], 4, 512), 2048,
                        (ada_unit, 4 * half + q + 1))

        n_y = 0
        moe_first = []
        ADA_MIXER = [(2, 3, 4, 5), (11,), (17,), (23,)]
        ADA_NORM = [(6,), (12,), (18,), ()]
        ADA_ROUTER = [(7,), (13,), (19,), ()]
        ADA_DISPATCH = [(8, 9), (14, 15), (20, 21), ()]
        ADA_END = [(10,), (16,), (22,), ()]
        hold = {}
        ada_units(0, 1)
        for L in range(LAYERS):
            kind, j = L % 3, L // 3
            ada_units(*ADA_MIXER[L])
            if kind == 0:
                add((A["w_pool"][j].rearrange("g c d -> (g c) d"), KC, 256), KC * 256, (y_full, n_y + 8))
            elif kind == 1:
                w = A["w_mlstm_in"][j]
                for i in range(4):
                    add((w[:, i * 256:(i + 1) * 256], KC, 256), 2048, (qk_full, 2 * (i + 1)))
                for i in range(4):
                    add((w[:, 1024 + i * 256:1024 + (i + 1) * 256], KC, 256), 2048, (v_full, NT * (i + 1)))
                for i in range(4):
                    add((w[:, 2048 + i * 256:2048 + (i + 1) * 256], KC, 256), 2048, (o_full, NT * (i + 1)))
                for i in range(4):
                    add((A["w_mlstm_out"][j][:, i * 256:(i + 1) * 256], KC, 256), 2048, (y_full, n_y + 2 * (i + 1)))
            else:
                w = A["w_mla_in"][j]
                for i in range(3):
                    add((w[:, i * 256:(i + 1) * 256], KC, 256), 2048, (pl_full, NT * (i + 1)))
                for i in range(4):
                    add((A["w_mla_qb"][j][:, i * 384:(i + 1) * 384], QL // P, 384), 1536, (qp_full, i + 1))
                for i in range(2):
                    add((A["w_mla_kvb"][j][:, i * 1024:(i + 1) * 1024], KVL // P, 1024), 2048, (vt_full, 4 * (i + 1)))
                for i in range(4):
                    add((A["w_mla_out"][j][:, i * 256:(i + 1) * 256], KC, 256), 2048, (y_full, n_y + 2 * (i + 1)))
            n_y += 8
            ada_units(*ADA_NORM[L], *ADA_ROUTER[L], *ADA_DISPATCH[L])
            moe_first.append(len(units))
            hold[len(units) + 4] = (xg_in[0], 16 * (NE // 2 * L + 1))
            hold[len(units) + 3 * NE + 6] = (yg_in[NT - 1], 32 * (L + 1))

            def gate_up(e):
                for n, name in enumerate(("w_exp_gate", "w_exp_up")):
                    add((A[name][L, e], KC, 256), 2048, (gu_full, 2 * (NE * L + e) + n + 1))

            def down(e):
                add((A["w_exp_down"][L, e], FE // P, D), 2048, (yp_full, 2 * (NE * L + e + 1)))

            gate_up(0)
            for e in range(1, NE):
                gate_up(e)
                down(e - 1)
            down(NE - 1)
            ada_units(*ADA_END[L])

        TURNS = (NE - 2) // UNROLL

        def arrived(eng, u):
            eng.wait_ge(slot_in[u % RING], 16 * (u // RING + 1))

        block = ctx.enter_context(nc.Block())

        @block.sync
        def _(sp):
            def load(u):
                src, n, _ = units[u]
                ap, k, c = src
                if u >= RING:
                    s, value = units[u - RING][2]
                    sp.wait_ge(s, value)
                if u in hold:
                    sp.wait_ge(*hold[u])
                sp.dma_start(slot(u)[:, 0:n].rearrange("p (k n) -> p k n", k=k),
                             ap.rearrange("(k p) n -> p k n", p=P)).then_inc(slot_in[u % RING], 16)

            sp.wait_ge(rows_loaded, 160)
            u = 0
            for L in range(LAYERS):
                first = moe_first[L] + 2
                while u < first + RING:
                    load(u)
                    u += 1
                with sp.Fori(1, TURNS) as it:
                    for b in range(RING):
                        _, _, (s, value) = units[first + b]
                        name = ("w_exp_gate", "w_exp_up", "w_exp_down")[b % 3]
                        e = it * UNROLL + b // 3 + (1 if b % 3 < 2 else 0)
                        k = KC if b % 3 < 2 else FE // P
                        sp.wait_ge(s, (it - 1) * (2 * UNROLL) + value)
                        sp.dma_start(slot(first + b).rearrange("p (k n) -> p k n", k=k),
                                     A[name][L, bass.ds(e, 1)].rearrange("e (k p) n -> p (e k) n", p=P))\
                          .then_inc(slot_in[(first + b) % RING], 16)
                u = first + TURNS * RING
            while u < len(units):
                load(u)
                u += 1
            assert u == len(units)

        @block.tensor
        def _(pe):
            def mm(out, lhsT, rhs, first, last):
                return pe.matmul(out, lhsT, rhs, start=first, stop=last)

            state = {"u": 0}

            def take():
                u = state["u"]
                state["u"] = u + 1
                arrived(pe, u)
                return slot(u)

            def ada(*halves):
                for half in halves:
                    first = half % 2 == 0
                    if first and half:
                        pe.wait_ge(mrow_ready, half // 2)
                        if bank_of.get(half // 2 - 1) == 7:
                            pe.wait_ge(mod_added, half // 2)
                    w = [take().rearrange("p (k n) -> p k n", k=4) for _ in range(4)]
                    for k in range(4):
                        for q in range(4):
                            ins = mm(ps[7][32 * q:32 * q + 2, :], cond[:, 4 * (half % 2) + k, :], w[q][:, k, :],
                                     first and k == 0, not first and k == 3)
                            if k == 3:
                                ins.then_inc(ada_unit, 1)

            bank_of = {}

            def ada_columns(g, bank):
                bank_of[g] = bank
                pe.wait_ge(mrow_ready, g + 1)
                for j in range(4):
                    ins = pe.transpose(ps[bank][:, j * P:(j + 1) * P], mrow[:, j * P:(j + 1) * P], ident[:, :])
                ins.then_inc(ada_full, 1)

            def norm(n):
                if n in (2, 4, 6):
                    pe.wait_ge(mod_added, 3 * (n // 2) + 2)
                for k in range(KC):
                    if k % 2 == 0:
                        pe.wait_ge(sq_ready, 4 * n + k // 2 + 1)
                    ins = mm(ps[6][:, 0:TOK], mean_ones[:, :], sq[:, k, :], k == 0, k == KC - 1)
                ins.then_inc(ms_full, 1)

            def project(r, src, ready, n_src):
                for i in range(4):
                    w = take().rearrange("p (k n) -> p k n", k=KC)
                    for b in range(2):
                        c = 2 * i + b
                        if c >= 4:
                            pe.wait_ge(x_ready, 8 * (r + 1) + c - 3)
                        for k in range(KC):
                            if c == 0:
                                pe.wait_ge(ready, n_src[k])
                            ins = mm(ps[c % 4][:, 0:TOK], w[:, k, b * P:(b + 1) * P], src[:, k, :], k == 0, k == KC - 1)
                        ins.then_inc(y_full, 1)

            def pool_mixer(r):
                w = take().rearrange("p (k n) -> p k n", k=KC)
                for c in range(KC):
                    g = c // 2
                    pe.wait_ge(pooled, 4 * (0 if r == 0 else 1) + g + 1)
                    if c >= 4:
                        pe.wait_ge(x_ready, 8 * (r + 1) + c - 3)
                    for k in range(2):
                        ins = mm(ps[c % 4][:, 0:TOK], w[:, 2 * g + k, (c % 2) * P:(c % 2 + 1) * P],
                                 hT[:, 2 * g + k, :], k == 0, k == 1)
                    ins.then_inc(y_full, 1)

            def mlstm(r):
                pe.wait_ge(h_ready, 16 * (r + 1))
                for t in range(NT):
                    for k in range(KC):
                        ins = mm(ps[4][:, t * 16:(t + 1) * 16], hT[:, k, t * P:(t + 1) * P], w_gt[:, k, :], k == 0, k == KC - 1)
                ins.then_inc(gate_full, 1)
                pe.wait_ge(gate_tok, 1)
                for g in range(4):
                    for t in range(NT):
                        ins = pe.transpose(ps[g][0:MH, t * P:(t + 1) * P], g_tok[:, t, g * 4:(g + 1) * 4], ident[:, :])
                ins.then_inc(grow_full, 1)
                for i in range(4):
                    w = take().rearrange("p (k n) -> p k n", k=KC)
                    for b in range(2):
                        c = 2 * i + b
                        if c >= 2:
                            pe.wait_ge(qk_ready, c - 1)
                        for k in range(KC):
                            ins = mm(ps[5 + c % 2][:, 0:TOK], w[:, k, b * P:(b + 1) * P], hT[:, k, :], k == 0, k == KC - 1)
                        ins.then_inc(qk_full, 1)
                for i in range(4):
                    w = take().rearrange("p (k n) -> p k n", k=KC)
                    for t in range(NT):
                        c = NT * i + t
                        if c >= 2:
                            pe.wait_ge(v_ready, c - 1)
                        else:
                            pe.wait_ge(qk_ready, 7 + c)
                        for k in range(KC):
                            ins = mm(ps[5 + c % 2][:, 0:DV], hT[:, k, t * P:(t + 1) * P], w[:, k, :], k == 0, k == KC - 1)
                        ins.then_inc(v_full, 1)
                pe.wait_ge(rows_done, 1)
                for d in range(2):
                    for q, src in enumerate((rA, rS, rE)):
                        for t in range(NT):
                            c = ((d * 3 + q) * NT + t) * MH
                            ins = pe.transpose(ps[4][:, 64 + c:64 + c + MH], src[:, d, t * P:(t + 1) * P], ident[0:MH, 0:MH])
                ins.then_inc(rowc_full, 1)
                for i in range(4):
                    w = take().rearrange("p (k n) -> p k n", k=KC)
                    for t in range(NT):
                        c = NT * i + t
                        pe.wait_ge(*((l_ready, c - 1) if c >= 2 else (v_ready, 11 + c)))
                        for k in range(KC):
                            ins = mm(ps[5 + c % 2][:, 0:DV], hT[:, k, t * P:(t + 1) * P], w[:, k, :], k == 0, k == KC - 1)
                        ins.then_inc(o_full, 1)
                pe.wait_ge(rowc_ready, 1)
                pe.wait_ge(state_set, 1)
                pe.wait_ge(state_in, 32)
                pe.wait_ge(vx_ones, 1)
                pe.wait_ge(tables_in, 32)
                pe.wait_ge(l_ready, 12)
                npj = 0
                for h in range(MH):
                    if h:
                        pe.wait_ge(at_ready, 3 * h)
                        pe.wait_ge(kk_ready, 2 * h)
                    for c, (s, t) in enumerate(((0, 0), (1, 1), (2, 2), (1, 2))):
                        mm(ps[0][:, c * P:(c + 1) * P], kT[:, h, s * P:(s + 1) * P], qT[:, h, t * P:(t + 1) * P], True, True)
                    mm(ps[1][:, 0:P], kT[:, h, 2 * P:3 * P], qT[:, h, P:2 * P], True, True)
                    pe.transpose(ps[1][:, P:2 * P], kT[:, h, 0:P], ident[:, :]).then_inc(s_full, 1)
                    for d in range(2):
                        if h:
                            pe.wait_ge(w_ready, 2 * (h - 1) + d + 1)
                        mm(ps[2 + d][:, 0:TOK], sel[:, h, :], rM[:, d, :], True, True).then_inc(mbc_full, 1)
                    for d in range(2):
                        if npj >= 3:
                            pe.wait_ge(p_used, npj - 2)
                        pe.wait_ge(kk_ready, 2 * h + d + 1)
                        mm(ps[4 + npj % 3][:, 0:VX], kkb[:, d, :], vx[:, 0, h, :], True, True).then_inc(p_full, 1)
                        npj += 1
                        pe.wait_ge(at_ready, 3 * h + (1 if d == 0 else 3))
                        for t in range(NT):
                            if npj >= 3:
                                pe.wait_ge(p_used, npj - 2)
                            b = ps[4 + npj % 3][:, 0:VX]
                            if t == 0 or (t == 1 and d == 0) or (t == 2 and d == 1):
                                mm(b, aT[:, d, t * P:(t + 1) * P], vx[:, t, h, :], True, True).then_inc(p_full, 1)
                            else:
                                mm(b, aT[:, d, t * P:(t + 1) * P], vx[:, t, h, :], True, False)
                                o = 2 if t == 1 else 1
                                mm(b, aT[:, d, 3 * P:4 * P], vx[:, o, h, :], False, True).then_inc(p_full, 1)
                            npj += 1
                            if t:
                                if npj >= 3:
                                    pe.wait_ge(p_used, npj - 2)
                                mm(ps[4 + npj % 3][:, 0:VX], qT[:, h, t * P:(t + 1) * P], cx[:, d, h, :], True, True)\
                                    .then_inc(p_full, 1)
                                npj += 1
                pe.wait_ge(p_used, npj)
                pe.transpose(ps[2][0:8, 0:P], nout, ident[:, :]).then_inc(nt_full, 1)
                pe.wait_ge(hn_ready, 12)
                for c in range(KC):
                    if c >= 2:
                        pe.wait_ge(hsT_ready, c - 1)
                    for t in range(NT):
                        ins = pe.transpose(ps[c % 2][:, t * P:(t + 1) * P],
                                           hs[:, t, c // 2, (c % 2) * P:(c % 2 + 1) * P], ident[:, :])
                    ins.then_inc(hsT_full, 1)
                pe.wait_ge(hsT_ready, 8)
                pe.wait_ge(n_copied, 1)
                project(r, hT, hsT_ready, [8] * KC)

            def mla(r):
                pe.wait_ge(h_ready, 16 * (r + 1))
                for i in range(4):
                    if i < 3:
                        w = take().rearrange("p (k n) -> p k n", k=KC)
                    else:
                        w = w_kp
                    n = 256 if i < 3 else ROPE
                    for t in range(NT):
                        c = NT * i + t
                        if c >= 4:
                            pe.wait_ge(pl_ready, c - 3)
                        for k in range(KC):
                            ins = mm(ps[c % 4][:, 0:n], hT[:, k, t * P:(t + 1) * P], w[:, k, :], k == 0, k == KC - 1)
                        ins.then_inc(pl_full, 1)
                pe.wait_ge(pn_ready, 3)
                pe.wait_ge(pl_ready, 12)
                for c in range(4):
                    for t in range(NT):
                        ins = pe.transpose(ps[c][:, t * P:(t + 1) * P], pl[:, t, c * P:(c + 1) * P], ident[:, :])
                    ins.then_inc(ql_full, 1)
                pe.wait_ge(pn_ready, 6)
                pe.wait_ge(cache_in, 48)
                for c in range(2):
                    for s in range(4):
                        src = cache[:, c * P:(c + 1) * P] if s == 1 else \
                            pl[:, max(s - 1, 0), QL + c * P:QL + (c + 1) * P]
                        ins = pe.transpose(ps[4 + c][:, s * P:(s + 1) * P], src, ident[:, :])
                    ins.then_inc(ck_full, 1)
                pe.wait_ge(kp_dup, 1)
                for s in range(4):
                    ins = pe.transpose(ps[6][:, s * P:(s + 1) * P], kp2[:, s, :], ident[:, :])
                ins.then_inc(kp_full, 1)
                pe.wait_ge(kp_ready, 1)
                pe.wait_ge(ql_ready, 4)
                mm(ps[6][:, 0:LAT], rot[:, :], kpT[:, KEYS - LAT:KEYS], True, True).then_inc(rot_full, 1)
                nq = 0
                for i in range(4):
                    w = take()[:, 0:1536].rearrange("p (k n) -> p k n", k=4)
                    for b in range(3):
                        if nq >= 4:
                            if (nq - 4) % 3 == 2:
                                pe.wait_ge(qp_raw, (nq - 4) // 3 + 1)
                            else:
                                pe.wait_ge(qn_ready, (nq - 4) // 3 * 2 + (nq - 4) % 3 + 1)
                        bank = ps[nq % 4][:, 0:TOK]
                        if b < 2:
                            for k in range(4):
                                ins = mm(bank, w[:, k, b * 192:b * 192 + NOPE], qlT[:, k, :], k == 0, k == 3)
                        else:
                            for o in range(2):
                                for k in range(4):
                                    ins = mm(bank[o * ROPE:(o + 1) * ROPE, :], w[:, k, o * 192 + NOPE:(o + 1) * 192],
                                             qlT[:, k, :], k == 0, k == 3)
                        ins.then_inc(qn_full if b < 2 else qp_full, 1)
                        nq += 1
                for i in range(4):
                    pe.wait_ge(qp_raw, i + 1)
                    pe.wait_ge(rope_ready, i + 1)
                    mm(ps[6][:, 0:LAT], rot[:, :], qpT[:, i, CTX:TOK], True, True).then_inc(rot_full, 1)
                pe.wait_ge(ck_ready, 2)
                for i in range(2):
                    w = take().rearrange("p (k n) -> p k n", k=2)
                    for b in range(4):
                        h = 4 * i + b
                        if h >= 2:
                            pe.wait_ge(kn_ready, h - 1)
                        else:
                            pe.wait_ge(qn_ready, 8)
                        for k in range(2):
                            ins = mm(ps[4 + h % 2][:, :], w[:, k, b * 256:b * 256 + NOPE], ckT[:, k, :], k == 0, k == 1)
                        ins.then_inc(kn_full, 1)
                    for s in range(4):
                        c = 4 * i + s
                        if c >= 4:
                            pe.wait_ge(vt_ready, c - 3)
                        else:
                            pe.wait_ge(qp_raw, 4)
                        for k in range(2):
                            rhs = w[:, k, :].rearrange("p (h n) -> p h n", h=4)[:, :, NOPE:]
                            ins = mm(ps[c % 4][:, :].rearrange("p (h n) -> p h n", h=4), ckT[:, k, s * P:(s + 1) * P],
                                     rhs, k == 0, k == 1)
                        ins.then_inc(vt_full, 1)
                pe.wait_ge(kn_ready, 8)
                pe.wait_ge(vt_ready, 8)
                pe.wait_ge(rope_ready, 5)
                def scores(h, t):
                    c = NT * h + t
                    if c >= 3:
                        pe.wait_ge(e_ready, c - 2)
                    lo, hi = (0, CTX) if t == 0 else (CTX, KEYS)
                    b = ps[c % 3][:, 0:hi - lo]
                    o = (h % 2) * ROPE
                    mm(b, qnT[:, h, t * P:(t + 1) * P], knT[:, h, lo:hi], True, False)
                    mm(b, qpT[o:o + ROPE, h // 2, t * P:(t + 1) * P], kpT[o:o + ROPE, lo:hi], False, True)\
                        .then_inc(sc_full, 1)

                for t in range(NT):
                    scores(0, t)
                for h in range(AH):
                    for t in range(NT):
                        c = NT * h + t
                        pe.wait_ge(p_ready, c + 1)
                        if h and t == 0:
                            pe.wait_ge(pt_ready, 2 * h)
                        if t == 0:
                            ins = pe.transpose(ps[4][:, 256:384], pr[:, c % 2, 0:P], ident[:, :])
                        else:
                            for s in range(3):
                                bank, o = (ps[3], s * 256) if s < 2 else (ps[4], 0)
                                ins = pe.transpose(bank[:, o + (t - 1) * P:o + t * P], pr[:, c % 2, s * P:(s + 1) * P], ident[:, :])
                        ins.then_inc(pt_full, 1)
                        if h + 1 < AH:
                            scores(h + 1, t)
                    pe.wait_ge(pt_ready, 2 * (h + 1))
                    if h >= 2:
                        pe.wait_ge(oT_ready, h - 1)
                    b = ps[5 + h % 2]
                    mm(b[:, 0:CTX], vt[:, 0, h, :], prT[:, 768:896], True, True)
                    for s in range(3):
                        ins = mm(b[:, CTX:TOK], vt[:, 1 + s, h, :], prT[:, s * 256:(s + 1) * 256], s == 0, s == 2)
                    ins.then_inc(o_att, 1)
                pe.wait_ge(oT_ready, 8)
                project(r, hT, oT_ready, [8] * KC)

            def experts(L, n):
                pe.wait_ge(h_ready, 16 * (n + 1))
                for t in range(NT):
                    for k in range(KC):
                        ins = mm(ps[6][:, t * NE:(t + 1) * NE], hT[:, k, t * P:(t + 1) * P], w_rt[:, k, :], k == 0, k == KC - 1)
                ins.then_inc(rt_full, 1)
                for c in range(2 * NT):
                    for k in range(4):
                        ins = pe.transpose(ps[c][:, k * P:(k + 1) * P],
                                           hT[:, 4 * (c % 2) + k, (c // 2) * P:(c // 2 + 1) * P], ident[:, :])
                    ins.then_inc(ht_full, 1)
                ada(*ADA_ROUTER[L])
                pe.wait_ge(mask_ready, L + 1)
                pick = rt[:, 5, :]
                for t in range(NT + 1):
                    for q in range(min(t, NT - 1) + 1):
                        ins = mm(ps[6][:, 64 + t * NE:64 + (t + 1) * NE], tri[:, :] if q == t else ones[:, :],
                                 pick[:, q * NE:(q + 1) * NE], q == 0, q == min(t, NT - 1))
                ins.then_inc(pos_full, 1)
                if L + 1 < LAYERS:
                    pe.wait_ge(ht_ready, 2 * NT * (L + 1))
                    ada(ADA_DISPATCH[L][0])
                    ada_columns(3 * (L + 1), 5)
                    ada(ADA_DISPATCH[L][1])
                u0 = moe_first[L]
                assert state["u"] == u0

                def turn_tokens(G, par):
                    pe.wait_ge(xg_in[par], G("in"))
                    for c in range(2):
                        for k in range(4):
                            ins = pe.transpose(ps[2 + c][:, k * P:(k + 1) * P], xg[:, par, (4 * c + k) * P:(4 * c + k + 1) * P],
                                               ident[:, :])
                        ins.then_inc(xt_full2, 1)

                def weights(u, it):
                    value = 16 * (u // RING + 1)
                    pe.wait_ge(slot_in[u % RING], value if it is None else it * 16 + value)
                    return slot(u)

                def gate_or_up(u, it, half, par):
                    w = weights(u + half, it).rearrange("p (k n) -> p k n", k=KC)
                    for k in range(KC):
                        ins = mm(ps[par][:, half * FE:(half + 1) * FE], xgT[:, par, k, :], w[:, k, :], k == 0, k == KC - 1)
                    ins.then_inc(gu_full, 1)

                def turn_hidden(G, par):
                    pe.wait_ge(hid_ready, G + 1)
                    for f in range(2):
                        ins = pe.transpose(ps[4][:, f * P:(f + 1) * P], hid[:, par, f * P:(f + 1) * P], ident[:, :])
                    ins.then_inc(hidT_full, 1)

                def down(u, it, G):
                    w = weights(u, it).rearrange("p (k n) -> p k n", k=2)
                    pe.wait_ge(hidT_ready, G + 1)
                    pe.wait_ge(yb_ready, G + 1)
                    for half in range(2):
                        for f in range(2):
                            ins = mm(ps[5 + half][:, :], hidT[:, f, :], w[:, f, half * 512:(half + 1) * 512], f == 0, f == 1)
                        ins.then_inc(yp_full, 1)

                def tokens_of(e, it):
                    v0 = 16 * ((NE * L + e) // 2 + 1)
                    turn_tokens(lambda _: v0 if it is None else it * (16 * UNROLL // 2) + v0, e % 2)

                def step(e, it):
                    G = NE * L + e if it is None else it * UNROLL + (NE * L + e)
                    pe.wait_ge(xa_ready, G + 1)
                    pe.wait_ge(xb_ready, G + 1)
                    gate_or_up(u0 + 2 + 3 * (e - 1), it, 0, e % 2)
                    turn_hidden(G - 1, (e - 1) % 2)
                    gate_or_up(u0 + 2 + 3 * (e - 1), it, 1, e % 2)
                    if e + 1 < NE:
                        tokens_of(e + 1, it)
                    down(u0 + 4 + 3 * (e - 1), it, G - 1)

                tokens_of(0, None)
                pe.wait_ge(xa_ready, NE * L + 1)
                pe.wait_ge(xb_ready, NE * L + 1)
                for half in range(2):
                    gate_or_up(u0, None, half, 0)
                tokens_of(1, None)
                with pe.Fori(0, TURNS) as it:
                    for e in range(1, 1 + UNROLL):
                        step(e, it)
                for e in range(1 + TURNS * UNROLL, NE):
                    step(e, None)
                turn_hidden(NE * L + NE - 1, 1)
                down(u0 + 3 * NE - 1, None, NE * L + NE - 1)
                state["u"] = u0 + 3 * NE
                ada(*ADA_END[L])
                for t in range(NT):
                    pe.wait_ge(ys_ready, NT * L + t + 1)
                    for c in range(2):
                        for k in range(4):
                            ins = pe.transpose(ps[2 * t + c][:, k * P:(k + 1) * P], yg[:, t, 0, (4 * c + k) * P:(4 * c + k + 1) * P],
                                               ident[:, :])
                        ins.then_inc(yc_full, 1)
                if L + 1 < LAYERS:
                    pe.wait_ge(yb_ready, NE * (L + 1) + 1)
                    ada_columns(3 * (L + 1) + 1, 6)
                pe.wait_ge(slots_ready, L + 1)
                over = pe.value_load(spill[0:1, 0:1], min_val=0, max_val=1)
                with pe.If(over > 0):
                    pe.wait_ge(f_comb, L + 1)
                    pe.wait_ge(x_ready, 8 * (n + 2))
                    for t in range(NT):
                        ins = pe.transpose(ps[4][0:NE, t * P:(t + 1) * P], rt[:, 11, t * NE:(t + 1) * NE], ident[:, :])
                    ins.then_inc(f_combT, 1)
                    pe.wait_ge(f_rows, 16 * (L + 1))
                    pe.wait_ge(f_zero, L + 1)
                    with pe.Fori(0, NE) as it:
                        G = it + NE * L
                        for half in range(2):
                            pe.wait_ge(f_w, G * 48 + 16 * (half + 1))
                            w = wF.rearrange("p (k n) -> p k n", k=KC)
                            for f in range(2):
                                for k in range(KC):
                                    ins = mm(ps[2 * half + f][:, 0:TOK], w[:, k, f * P:(f + 1) * P], hT[:, k, :], k == 0, k == KC - 1)
                                ins.then_inc(f_gu, 1)
                        mm(ps[4][:, 0:TOK], ones[0:1, :], comb_row[0:1, bass.ds(it, 1), :].rearrange("p e t -> p (e t)"),
                           True, True).then_inc(f_cb, 1)
                        pe.wait_ge(f_w, G * 48 + 48)
                        pe.wait_ge(f_hid, G * 2 + 2)
                        w = wF.rearrange("p (k n) -> p k n", k=2)
                        for c in range(KC):
                            if c >= 2:
                                pe.wait_ge(f_yused, G * 8 + (c - 1))
                            for f in range(2):
                                ins = mm(ps[5 + c % 2][:, 0:TOK], w[:, f, c * P:(c + 1) * P], hidF[:, f, :], f == 0, f == 1)
                            ins.then_inc(f_y, 1)
                with pe.Else():
                    pe.sem_inc(f_combT, 1)
                    pe.sem_inc(f_gu, 4 * NE)
                    pe.sem_inc(f_cb, NE)
                    pe.sem_inc(f_y, 8 * NE)

            pe.wait_ge(ident_in, 16)
            pe.wait_ge(rows_loaded, 160)
            pe.wait_ge(pool_set, 3)
            pe.transpose(ps[6][:, 0:124], rows_in[0:124, 0, :], ident[0:124, 0:124])
            pe.transpose(ps[6][:, 128:224], rows_in[0:96, 1, :], ident[0:96, 0:96])
            pe.transpose(ps[6][:, 256:352], rows_in[0:96, 2, :], ident[0:96, 0:96]).then_inc(vec_t, 1)
            pe.wait_ge(x_loaded, 16 * NT)
            for c in range(KC):
                if c >= 4:
                    pe.wait_ge(x_ready, c - 3)
                for t in range(NT):
                    ins = pe.transpose(ps[c % 4][:, t * P:(t + 1) * P], x_in[:, t, c * P:(c + 1) * P], ident[:, :])
                ins.then_inc(xt_full, 1)
            pe.wait_ge(cond_ready, 2)
            pe.wait_ge(bank7_set, 1)
            ada(0, 1)
            ada_columns(0, 5)
            for L in range(LAYERS):
                norm(2 * L)
                if L == 0:
                    ada(2, 3)
                    pe.wait_ge(mod_added, 1)
                    ada_columns(1, 5)
                    ada(4, 5)
                else:
                    ada(*ADA_MIXER[L])
                (pool_mixer, mlstm, mla)[L % 3](2 * L)
                ada_columns(3 * L + 2, 7)
                if L == 0:
                    pe.wait_ge(const_in, 16 * NCONST)
                norm(2 * L + 1)
                ada(*ADA_NORM[L])
                experts(L, 2 * L + 1)
            norm(2 * LAYERS)
            for t in range(NT):
                for half in range(2):
                    c = 2 * t + half
                    pe.wait_ge(h_scaled, 16 * (2 * LAYERS + 1))
                    if c >= 4:
                        pe.wait_ge(yt_ready, c - 3)
                    for k in range(4):
                        ins = pe.transpose(ps[c % 4][:, k * P:(k + 1) * P], hT[:, 4 * half + k, t * P:(t + 1) * P], ident[:, :])
                    ins.then_inc(yt_full, 1)

        @block.scalar
        def _(act):
            n_step = {"n": 0}

            def step(ins):
                ins.then_inc(act_step, 1)
                n_step["n"] += 1

            def settle():
                act.wait_ge(act_step, n_step["n"])

            act.dma_start(ident[:, :], A["k_ident"]).then_inc(ident_in, 16)
            act.dma_start(rows_in[0:8, 0, :], A["c_ctx"].rearrange("(r n) -> r n", n=P)).then_inc(rows_loaded, 16)
            act.dma_start(rows_in[8:16, 0, :], A["c"].rearrange("a (r n) -> (a r) n", n=P)).then_inc(rows_loaded, 16)
            act.dma_start(rows_in[16:48, 0, :], A["norm_mix"].rearrange("l (r n) -> (l r) n", n=P)).then_inc(rows_loaded, 16)
            act.dma_start(rows_in[48:80, 0, :], A["norm_ffn"].rearrange("l (r n) -> (l r) n", n=P)).then_inc(rows_loaded, 16)
            act.dma_start(rows_in[80:88, 0, :], A["norm_final"].rearrange("(r n) -> r n", n=P)).then_inc(rows_loaded, 16)
            act.dma_start(rows_in[88:104, 0, :], A["pool_scale"].rearrange("l (r n) -> (l r) n", n=P)).then_inc(rows_loaded, 16)
            act.dma_start(rows_in[104:112, 0, :], A["mlstm_head_g"].rearrange("l (r n) -> (l r) n", n=P)).then_inc(rows_loaded, 16)
            act.dma_start(rows_in[112:116, 0, :], A["mla_q_g"].rearrange("l (r n) -> (l r) n", n=P)).then_inc(rows_loaded, 16)
            act.dma_start(rows_in[116:124, 0, :], A["state_mlstm_n"].rearrange("b l s h k -> (b l s h) k")).then_inc(rows_loaded, 16)
            act.dma_start(rows_in[0:96, 1:3, :],
                          A["b_ada"].rearrange("l (r n) -> (l r) n", n=P).rearrange("(a r) n -> r a n", a=2)).then_inc(rows_loaded, 16)
            for t in range(NT):
                src = A["x_prompt"][0] if t == 0 else A["x_sample"][0, (t - 1) * P:t * P]
                act.dma_start(x_in[:, t, :], src).then_inc(x_loaded, 16)
            act.dma_start(trig[:, :, :], A["k_trig"]).then_inc(const_in, 16)
            act.dma_start(rot[:, :], A["k_rot"]).then_inc(const_in, 16)
            act.dma_start(tri[:, :], A["k_tri"]).then_inc(const_in, 16)
            act.dma_start(base[:, :], A["k_base"].partition_broadcast(P)).then_inc(const_in, 16)
            act.dma_start(w_rt[:, :, :], A["w_router"].rearrange("(k p) n -> p k n", p=P)).then_inc(const_in, 16)
            act.dma_start(w_gt[:, :, :], A["w_mlstm_in"][0, :, 3072:3088].rearrange("(k p) n -> p k n", p=P)).then_inc(const_in, 16)
            act.dma_start(w_kp[:, :, :], A["w_mla_in"][0, :, 768:832].rearrange("(k p) n -> p k n", p=P)).then_inc(const_in, 16)
            act.dma_start(b_rt[:, :], A["b_router"].partition_broadcast(P)).then_inc(const_in, 16)
            act.dma_start(b_gt[:, :], A["b_mlstm_gate"].rearrange("l a h -> (l a h)").partition_broadcast(P)).then_inc(const_in, 16)
            act.dma_start(g_kv[:, :], A["mla_kv_g"][0].partition_broadcast(P)).then_inc(const_in, 16)
            with nc.allow_non_contiguous_dma(reason="eight floats"):
                act.dma_start(m0[:, :], A["state_mlstm_m"].rearrange("b l s h -> h (b l s)")).then_inc(const_in, 16)

            act.wait_ge(vec_cols, 1)
            cc = vecs[:, 0:16].rearrange("p (c k) -> p k c", c=2)
            act.activation(cond[:, :, :], cc, ACT.Exp, scale=-1.0).then_inc(cond_ready, 1)

            def mod_rows(g):
                act.wait_ge(ada_unit, 8 * (g + 1))
                if g:
                    act.wait_ge(ada_full, g)
                act.activation(mrow[:, :], ps[7][:, :], ACT.Copy).then_inc(mrow_ready, 1)

            def norm(n, bias, out):
                if n and n % 2 == 0:
                    act.wait_ge(spill_done, n // 2)
                for k in range(4):
                    act.wait_ge(x_ready, 8 * (n + 1) - 6 + 2 * k)
                    if n:
                        act.wait_ge(ms_full, n)
                    act.activation(sq[:, 2 * k:2 * k + 2, :], xT[:, 2 * k:2 * k + 2, :], ACT.Square).then_inc(sq_ready, 1)
                act.wait_ge(ms_full, n + 1)
                if n:
                    act.wait_ge(h_scaled, 16 * n)
                step(act.activation(rstd[:, :], ps[6][:, 0:TOK], ACT.Ln, bias=eps[:, 0:1]))
                settle()
                act.activation(rstd[:, :], rstd[:, :], ACT.Exp, scale=-0.5).then_inc(rstd_ready, 1)
                if bias is None:
                    return
                for k in range(KC):
                    for c in range(2):
                        act.wait_ge(h_scaled, 16 * n + 2 * k + c + 1)
                        o = out(k, c)
                        act.activation(o, hT[:, k, SPAN[c][0]:SPAN[c][1]], ACT.Identity, bias=bias[:, k, c:c + 1]).then_inc(h_ready, 1)

            def h_out(k, c):
                return hT[:, k, SPAN[c][0]:SPAN[c][1]]

            def hp_out(k, c):
                return hp[:, k, HP_AT[c]:HP_AT[c] + SPAN[c][1] - SPAN[c][0]]

            def mlstm(r):
                act.wait_ge(grow_full, 1)
                for d in range(2):
                    step(act.activation(rB[:, d, :], ps[2 * d + 1][0:MH, 0:TOK], ACT.Abs))
                settle()
                step(act.activation(rB, rB, ACT.Exp, scale=-1.0))
                settle()
                act.activation(rI, rB, ACT.Ln, bias=1.0).then_inc(softplus, 1)
                for c in range(8):
                    act.wait_ge(qk_full, c + 1)
                    dst = (qT if c < 4 else kT)[:, c % 4, :]
                    act.activation(dst, ps[5 + c % 2][:, 0:TOK], ACT.Copy, scale=float(DK ** -0.5) if c < 4 else 1.0).then_inc(qk_ready, 1)
                for c in range(12):
                    act.wait_ge(v_full, c + 1)
                    act.activation(vx[:, c % 3, c // 3, 0:DV], ps[5 + c % 2][:, 0:DV], ACT.Copy).then_inc(v_ready, 1)
                for c in range(12):
                    act.wait_ge(o_full, c + 1)
                    act.activation(og[:, c % 3, c // 3, :], ps[5 + c % 2][:, 0:DV], ACT.Exp, scale=-1.0).then_inc(l_ready, 1)
                act.wait_ge(rowc_set, 1)
                rc = small[:, 48:120].rearrange("p (d n) -> p d n", d=2)[:, :, 12:36]
                act.activation(rc, rc, ACT.Exp, scale=-1.0).then_inc(rowc_ready, 1)
                act.wait_ge(rowc_ready, 1)
                last_p1 = 0
                npj = 0
                for h in range(MH):
                    for d in range(2):
                        act.wait_ge(mm_ready, 2 * h + d + 1)
                        if h:
                            act.wait_ge(at_ready, 3 * h)
                            act.wait_ge(kk_ready, 2 * h)
                        for s in range(NT):
                            act.activation(wgt[:, d, s * P:(s + 1) * P], mm_[:, d, s * P:(s + 1) * P], ACT.Exp, scale=-1.0,
                                           bias=rowc[:, d, 0, s, h:h + 1])
                        s, t = (1, 2) if d == 0 else (2, 1)
                        act.activation(wgt[:, d, 3 * P:4 * P], ps[2 + d][:, t * P:(t + 1) * P], ACT.Exp, scale=-1.0,
                                       bias=rowc[:, d, 0, s, h:h + 1]).then_inc(w_ready, 1)
                    for d in range(2):
                        npj += 1
                        for t in range(NT):
                            npj += 1
                            if t:
                                npj += 1
                                act.wait_ge(p_full, npj)
                                if last_p1:
                                    act.wait_ge(p_used, last_p1)
                                last_p1 = npj
                                act.activation(p1s, ps[4 + (npj - 1) % 3][:, 0:VX], ACT.Copy, scale=rowc[:, d, 1, t, h:h + 1])\
                                   .then_inc(p1_ready, 1)
                for h in range(MH):
                    for t in range(NT):
                        act.wait_ge(ss_ready, 12)
                        act.activation(mm_[:, 0, 0:DV], hs[:, t, h, :], ACT.Square,
                                       accum_out=ssq[:, NT * h + t:NT * h + t + 1]).then_inc(act_step, 1)
                        n_step["n"] += 1
                        settle()
                step(act.activation(hrs, ssq, ACT.Ln, scale=1.0 / DV, bias=eps[:, 0:1]))
                settle()
                act.activation(hrs, hrs, ACT.Exp, scale=-0.5).then_inc(hrs_ready, 1)
                for c in range(KC):
                    act.wait_ge(hsT_full, c + 1)
                    act.activation(hT[:, c, :], ps[c % 2][:, 0:TOK], ACT.Copy, scale=vecs[:, 104 + c:105 + c]).then_inc(hsT_ready, 1)

            def mla(r):
                for c in range(12):
                    i, t = c // 3, c % 3
                    act.wait_ge(pl_full, c + 1)
                    n = 256 if i < 3 else ROPE
                    act.activation(pl[:, t, i * 256:i * 256 + n], ps[c % 4][:, 0:n], ACT.Copy).then_inc(pl_ready, 1)
                act.wait_ge(pl_ready, 12)
                for t in range(NT):
                    step(act.activation(knT[:, 0, :], pl[:, t, 0:QL], ACT.Square, accum_out=acol[:, t:t + 1]))
                    settle()
                for t in range(NT):
                    step(act.activation(knT[:, 0, 0:KVL], pl[:, t, QL:QL + KVL], ACT.Square, accum_out=acol[:, 3 + t:4 + t]))
                    settle()
                step(act.activation(acol[:, 6:9], acol[:, 0:3], ACT.Ln, scale=1.0 / QL, bias=eps[:, 0:1]))
                step(act.activation(acol[:, 9:12], acol[:, 3:6], ACT.Ln, scale=1.0 / KVL, bias=eps[:, 0:1]))
                settle()
                act.activation(acol[:, 12:18], acol[:, 6:12], ACT.Exp, scale=-0.5).then_inc(prs_ready, 1)
                for c in range(4):
                    act.wait_ge(ql_full, c + 1)
                    act.activation(qlT[:, c, :], ps[c][:, 0:TOK], ACT.Copy, scale=vecs[:, 112 + c:113 + c]).then_inc(ql_ready, 1)
                for c in range(2):
                    act.wait_ge(ck_full, c + 1)
                    act.activation(ckT[:, c, :], ps[4 + c][:, :], ACT.Copy).then_inc(ck_ready, 1)
                nq = 0
                for i in range(4):
                    for b in range(2):
                        act.wait_ge(qn_full, 2 * i + b + 1)
                        act.activation(qnT[:, 2 * i + b, :], ps[nq % 4][:, 0:TOK], ACT.Copy).then_inc(qn_ready, 1)
                        nq += 1
                    nq += 1
                for i in range(2):
                    for b in range(4):
                        h = 4 * i + b
                        act.wait_ge(kn_full, h + 1)
                        act.activation(knT[:, h, :], ps[4 + h % 2][:, :], ACT.Copy).then_inc(kn_ready, 1)
                for c in range(NT * AH):
                    h, t = c // NT, c % NT
                    n = CTX if t == 0 else KEYS - CTX
                    act.wait_ge(mx_ready, c + 1)
                    if c >= 2:
                        act.wait_ge(pt_full, c - 1)
                    act.activation(pr[:, c % 2, 0:n], ps[c % 3][:, 0:n], ACT.Exp, scale=SCALE, bias=acol[:, 20 + c % 4:21 + c % 4],
                                   accum_out=acol[:, 24 + c % 4:25 + c % 4]).then_inc(e_ready, 1)
                    if t == NT - 1:
                        act.wait_ge(pt_full, NT * (h + 1))
                        if h:
                            act.wait_ge(o_att, h)
                        act.activation(prT[:, 0:512], ps[3][:, :], ACT.Copy).then_inc(pt_ready, 1)
                        act.activation(prT[:, 512:896], ps[4][:, 0:384], ACT.Copy).then_inc(pt_ready, 1)

            def experts(L, n):
                act.wait_ge(rt_full, L + 1)
                act.activation(rt[:, 1, :], ps[6][:, 0:48], ACT.Exp, scale=-1.0).then_inc(rt_e, 1)
                for c in range(2 * NT):
                    act.wait_ge(ht_full, 2 * NT * L + c + 1)
                    act.activation(htok[:, c // 2, (c % 2) * 512:(c % 2 + 1) * 512], ps[c][:, :], ACT.Copy).then_inc(ht_ready, 1)

                if L + 1 < LAYERS:
                    mod_rows(3 * (L + 1))
                    mod_rows(3 * (L + 1) + 1)

                def tokens_of(G, par):
                    act.wait_ge(xt_full2, G * 2 + 1)
                    act.activation(xgT[:, par, 0:4, :].rearrange("p k s -> p (k s)"), ps[2][:, :], ACT.Copy).then_inc(xa_ready, 1)

                def silu(G, par):
                    act.wait_ge(gu_full, G * 2 + 2)
                    act.activation(sil[:, par, :], ps[par][:, 0:FE], ACT.Silu).then_inc(sil_ready, 1)

                def turned(G):
                    act.wait_ge(hidT_full, G + 1)
                    act.activation(hidT.rearrange("p f s -> p (f s)"), ps[4][:, 0:FE], ACT.Copy).then_inc(hidT_ready, 1)

                def out(G, par, stored):
                    act.wait_ge(yp_full, G * 2 + 1)
                    act.wait_ge(y_stored[par], stored)
                    act.activation(ysb[:, par, 0:512], ps[5][:, :], ACT.Copy).then_inc(ya_ready, 1)

                def step(e, it):
                    G = NE * L + e if it is None else it * UNROLL + (NE * L + e)
                    turned(G - 1)
                    silu(G, e % 2)
                    if e + 1 < NE:
                        tokens_of(G + 1, (e + 1) % 2)
                    s0 = 16 * ((NE * L + e - 1) // 2 + 1)
                    out(G - 1, (e - 1) % 2, s0 if it is None else it * (8 * UNROLL) + s0)

                tokens_of(NE * L, 0)
                silu(NE * L, 0)
                tokens_of(NE * L + 1, 1)
                with act.Fori(0, TURNS) as it:
                    for e in range(1, 1 + UNROLL):
                        step(e, it)
                for e in range(1 + TURNS * UNROLL, NE):
                    step(e, None)
                turned(NE * L + NE - 1)
                out(NE * L + NE - 1, 1, 16 * ((NE * L + NE - 1) // 2 + 1))
                for t in range(NT):
                    act.wait_ge(yg_in[t], 32 * (L + 1))
                    act.activation(yg[:, t, 0, :], yg[:, t, 0, :], ACT.Copy, scale=rt[:, 12, t:t + 1]).then_inc(yw_ready, 1)
                act.wait_ge(slots_ready, L + 1)
                over = act.value_load(spill[0:1, 0:1], min_val=0, max_val=1)
                with act.If(over > 0):
                    with act.Fori(0, NE) as it:
                        G = it + NE * L
                        for f in range(2):
                            act.wait_ge(f_gu, G * 4 + (f + 1))
                            act.activation(sg[:, f, :], ps[f][:, 0:TOK], ACT.Silu).then_inc(f_sg, 1)
                with act.Else():
                    act.sem_inc(f_sg, 2 * NE)

            mod_rows(0)
            for L in range(LAYERS):
                kind = L % 3
                act.wait_ge(mod_added, 3 * L + 1)
                norm(2 * L, mod[:, L, 0:8, :], hp_out if kind == 0 else h_out)
                if L == 0:
                    mod_rows(1)
                mod_rows(3 * L + 2)
                if kind == 1:
                    mlstm(2 * L)
                elif kind == 2:
                    mla(2 * L)
                act.wait_ge(mod_added, 3 * L + 2)
                norm(2 * L + 1, mod[:, L, 24:32, :], h_out)
                experts(L, 2 * L + 1)
            norm(2 * LAYERS, None, None)
            for c in range(6):
                act.wait_ge(yt_full, c + 1)
                act.activation(yacc[:, :, :].rearrange("p k t -> p (k t)")[:, c * 512:(c + 1) * 512], ps[c % 4][:, :], ACT.Copy)\
                   .then_inc(yt_ready, 1)
            act.wait_ge(yt_ready, 6)
            y = yacc[:, :, :].rearrange("p k t -> p (k t)").rearrange("p (t d) -> p t d", t=NT)
            for t in range(NT):
                dst = O["y_prompt"][0] if t == 0 else O["y_sample"][0, (t - 1) * P:t * P]
                act.dma_start(dst, y[:, t, :]).then_inc(out_y, 16)
            act.wait_ge(out_y, 16 * NT)

        @block.vector
        def _(v):
            n_step = {"n": 0}

            def step(ins):
                ins.then_inc(vec_step, 1)
                n_step["n"] += 1

            def settle():
                v.wait_ge(vec_step, n_step["n"])

            v.memset(ps[7][:, :], 0.0).then_inc(bank7_set, 1)
            v.memset(hid[:, 0, 0:1], 0.0).then_inc(yb_ready, 1)
            v.wait_ge(vec_t, 1)
            v.tensor_copy(vecs[:, :], ps[6][:, 0:124]).then_inc(vec_cols, 1)
            for a in range(2):
                v.tensor_copy(b_ada[:, 96 * a:96 * (a + 1)], ps[6][:, 128 * (a + 1):128 * (a + 1) + 96]).then_inc(vec_cols, 1)
            v.wait_ge(vec_cols, 3)
            v.wait_ge(cond_ready, 1)
            cc = vecs[:, 0:16].rearrange("p (c k) -> p k c", c=2)
            step(v.tensor_scalar(cond[:, :, :], cond[:, :, :], 1.0, None, ALU.add)); settle()
            step(v.reciprocal(cond[:, :, :], cond[:, :, :])); settle()
            v.tensor_tensor(cond[:, :, :], cond[:, :, :], cc, ALU.mult).then_inc(cond_ready, 1)
            for c in range(KC):
                v.wait_ge(xt_full, c + 1)
                v.tensor_copy(xT[:, c, :], ps[c % 4][:, 0:TOK]).then_inc(x_ready, 1)

            def mod_columns(n, bank):
                L, g = n // 3, n % 3
                v.wait_ge(ada_full, n + 1)
                cols = ps[bank][:, :].rearrange("p (j q c) -> p q j c", j=4, q=4)[:, :, :, 0:2]
                v.tensor_tensor(mod[:, L, 16 * g:16 * (g + 1), :].rearrange("p (q j) c -> p q j c", q=4), cols,
                                b_ada[:, 48 * L + 16 * g:48 * L + 16 * (g + 1)].rearrange("p (q j) -> p q j", q=4)
                                .unsqueeze(3).to_broadcast([P, 4, 4, 2]), ALU.add).then_inc(mod_added, 1)
                v.wait_ge(mod_added, n + 1)
                if g == 1 and L % 3 == 0:
                    j = L // 3
                    step(v.tensor_tensor(gpool[:, :, :], mod[:, L, 16:24, :],
                                         vecs[:, 88 + 8 * j:96 + 8 * j].unsqueeze(2).to_broadcast([P, KC, 2]), ALU.mult))
                elif g != 1:
                    a, m, o = (0, 8, 16) if g == 0 else (1, 32, 48)
                    gain = vecs[:, o + 8 * L:o + 8 * L + 8].unsqueeze(2).to_broadcast([P, KC, 2])
                    step(v.scalar_tensor_tensor(out=amp[:, a, :, :], in0=mod[:, L, m:m + 8, :], scalar=1.0, in1=gain,
                                                op0=ALU.add, op1=ALU.mult))
                settle()

            def norm(n, gain):
                v.wait_ge(rstd_ready, n + 1)
                for k in range(KC):
                    for c in range(2):
                        a, b = SPAN[c]
                        g = gain[:, k, c:c + 1] if len(gain.shape) == 3 else gain[:, k:k + 1]
                        v.scalar_tensor_tensor(out=hT[:, k, a:b], in0=xT[:, k, a:b], scalar=g, in1=rstd[:, a:b],
                                               op0=ALU.mult, op1=ALU.mult).then_inc(h_scaled, 1)

            def residual(r, gate, src, wait):
                for c in range(KC):
                    if wait is not None:
                        v.wait_ge(y_full, wait + c + 1)
                    for q in range(2):
                        a, b = SPAN[q]
                        ins = v.scalar_tensor_tensor(out=xT[:, c, a:b], in0=src(c)[:, a:b], scalar=gate[:, c, q:q + 1],
                                                     in1=xT[:, c, a:b], op0=ALU.mult, op1=ALU.add)
                    ins.then_inc(x_ready, 1)

            def pool_mixer(r):
                v.wait_ge(h_ready, 16 * (r + 1))
                v.wait_ge(pads_set, 3 if r == 0 else 6)
                add = lambda o, a, b: v.tensor_tensor(o, a, b, ALU.add)
                step(add(ping[:, :, 1:HP], hp[:, :, 0:HP - 1], hp[:, :, 1:HP])); settle()
                step(add(pong[:, 2:8, 2:HP - 1], ping[:, 2:8, 1:HP - 2], ping[:, 2:8, 3:HP])); settle()
                step(add(ping[:, 4:8, 4:HP - 3], pong[:, 4:8, 2:HP - 5], pong[:, 4:8, 6:HP - 1])); settle()
                step(add(pong[:, 6:8, 8:HP - 7], ping[:, 6:8, 4:HP - 11], ping[:, 6:8, 12:HP - 3])); settle()
                if r == 0:
                    mod_columns(1, 5)
                v.wait_ge(inv_in, 16 if r == 0 else 32)
                for g in range(4):
                    src = (ping, pong)[g % 2]
                    for q in range(2):
                        a, b = SPAN[q]
                        o = HP_AT[q]
                        iv = inv[:, g, a:b].unsqueeze(1).to_broadcast([P, 2, b - a])
                        step(v.tensor_tensor(hT[:, 2 * g:2 * g + 2, a:b], src[:, 2 * g:2 * g + 2, o:o + b - a], iv, ALU.mult))
                    settle()
                    for q in range(2):
                        a, b = SPAN[q]
                        o = HP_AT[q]
                        ins = v.tensor_tensor(hT[:, 2 * g:2 * g + 2, a:b], hT[:, 2 * g:2 * g + 2, a:b],
                                              hp[:, 2 * g:2 * g + 2, o:o + b - a], ALU.subtract)
                    ins.then_inc(pooled, 1)

            def mlstm(r):
                v.tensor_copy(cx[:, :, :, DV:VX].rearrange("p d h o -> p (d h o)"), vecs[:, 116:124]).then_inc(state_set, 1)
                v.wait_ge(gate_full, 1)
                v.tensor_tensor(g_tok, ps[4][:, 0:48].rearrange("p (t g) -> p t g", t=NT),
                                b_gt[:, :].unsqueeze(1).to_broadcast([P, NT, 16]), ALU.add).then_inc(gate_tok, 1)
                v.wait_ge(grow_full, 1)
                v.wait_ge(softplus, 1)
                for d in range(2):
                    step(v.scalar_tensor_tensor(out=rI[:, d, :], in0=ps[2 * d + 1][0:MH, 0:TOK], scalar=0.0, in1=rI[:, d, :],
                                                op0=ALU.min, op1=ALU.subtract))
                settle()

                def seq(row, d, q):
                    a, b = SPAN[q]
                    s = row[:, d, a:b]
                    return s if d == 0 else s[:, ::-1]

                for d in range(2):
                    for q in range(2):
                        n = SPAN[q][1] - SPAN[q][0]
                        step(v.tensor_tensor_scan(seq(rB, d, q), ones[0:MH, 0:1].to_broadcast([MH, n]), seq(rI, d, q),
                                                  0.0, ALU.mult, ALU.add))
                settle()
                for d in range(2):
                    step(v.tensor_tensor(rA[:, d, :], ps[2 * d][0:MH, 0:TOK], rB[:, d, :], ALU.subtract))
                settle()
                for d in range(2):
                    for q in range(2):
                        step(v.tensor_tensor_scan(seq(rM, d, q), seq(rA, d, q), seq(rA, d, q),
                                                  0.0 if q == 0 else m0[:, d:d + 1], ALU.max, ALU.max))
                settle()
                step(v.tensor_tensor(rE[:, :, :], rM[:, :, :], rB, ALU.add))
                settle()
                v.tensor_copy(rS[:, :, 0:CTX], rM[:, :, 0:CTX])
                for d in range(2):
                    ins = v.tensor_scalar(rS[:, d, CTX:TOK], rM[:, d, CTX:TOK], m0[:, d:d + 1], None, ALU.subtract)
                ins.then_inc(rows_done, 1)
                v.wait_ge(rowc_full, 1)
                v.tensor_copy(rowc.rearrange("p d k t h -> p (d k t h)"), ps[4][:, 64:136]).then_inc(rowc_set, 1)
                for i in range(MH):
                    for t in range(NT):
                        v.wait_ge(l_ready, NT * i + t + 1)
                        o = og[:, t, i, :]
                        step(v.tensor_scalar(o, o, 1.0, None, ALU.add)); settle()
                        v.reciprocal(o, o).then_inc(o_ready, 1)
                npj = 0
                nl = n_hs = 0
                v.wait_ge(tables_in, 32)
                for h in range(MH):
                    for d in range(2):
                        v.wait_ge(mbc_full, 2 * h + d + 1)
                        if h:
                            v.wait_ge(w_ready, 2 * h)
                        v.tensor_tensor(mm_[:, d, :].rearrange("p (b t) -> p b t", b=NT),
                                        ps[2 + d][:, 0:TOK].rearrange("p (b t) -> p b t", b=NT),
                                        mask[:, d, :].unsqueeze(1).to_broadcast([P, NT, P]), ALU.add).then_inc(mm_ready, 1)
                    v.wait_ge(s_full, h + 1)
                    if h:
                        v.wait_ge(p_full, npj)
                    for d in range(2):
                        v.wait_ge(w_ready, 2 * h + d + 1)
                        col = wgt[:, d, P - 1:P] if d == 0 else wgt[:, d, 0:1]
                        v.tensor_scalar(kkb[:, d, :], ps[1][:, P:2 * P], col, None, ALU.mult).then_inc(kk_ready, 1)
                        if d == 0:
                            v.tensor_tensor(aT[:, 0, :], wgt[:, 0, :], ps[0][:, :], ALU.mult).then_inc(at_ready, 1)
                        else:
                            v.tensor_tensor(aT[:, 1, 0:TOK], wgt[:, 1, 0:TOK], ps[0][:, 0:TOK], ALU.mult).then_inc(at_ready, 1)
                            v.tensor_tensor(aT[:, 1, TOK:512], wgt[:, 1, TOK:512], ps[1][:, 0:P], ALU.mult).then_inc(at_ready, 1)
                    for d in range(2):
                        npj += 1
                        v.wait_ge(p_full, npj)
                        if h or d:
                            v.wait_ge(out_c, 16 * (2 * h + d))
                        v.tensor_copy(c_st[:, :], ps[4 + (npj - 1) % 3][:, 0:DV]).then_inc(c_copied, 1)
                        v.tensor_copy(nout[:, MH * d + h:MH * d + h + 1], ps[4 + (npj - 1) % 3][:, DV:VX]).then_inc(p_used, 1)
                        for t in range(NT):
                            npj += 1
                            v.wait_ge(p_full, npj)
                            p2 = ps[4 + (npj - 1) % 3][:, 0:VX]
                            if n_hs:
                                v.wait_ge(ss_ready, n_hs)
                            if t == 0:
                                v.tensor_copy(nd, p2).then_inc(p_used, 1)
                            else:
                                npj += 1
                                nl += 1
                                v.wait_ge(p1_ready, nl)
                                v.tensor_tensor(nd, p1s, p2, ALU.add).then_inc(p_used, 2)
                            v.wait_ge(p_used, npj)
                            en = rowc[:, d, 2, t, h:h + 1]
                            den = nd[:, DV:VX]
                            step(v.scalar_tensor_tensor(out=dcol[:, 2:3], in0=den, scalar=-1.0, in1=den,
                                                        op0=ALU.mult, op1=ALU.max)); settle()
                            step(v.tensor_tensor(dcol[:, 0:1], dcol[:, 2:3], en, ALU.max)); settle()
                            step(v.reciprocal(dcol[:, 1:2], dcol[:, 0:1])); settle()
                            o = hs[:, t, h, :]
                            if d == 0:
                                step(v.tensor_scalar(o, nd[:, 0:DV], dcol[:, 1:2], None, ALU.mult)); settle()
                            else:
                                v.scalar_tensor_tensor(out=o, in0=nd[:, 0:DV], scalar=dcol[:, 1:2], in1=o,
                                                       op0=ALU.mult, op1=ALU.add).then_inc(ss_ready, 1)
                                n_hs += 1
                v.wait_ge(nt_full, 1)
                v.tensor_copy(n_t[0:8, :], ps[2][0:8, 0:P]).then_inc(n_copied, 1)
                v.wait_ge(hrs_ready, 1)
                v.wait_ge(out_c, 16 * 8)
                v.wait_ge(out_m, 32)
                v.wait_ge(o_ready, 12)
                for h in range(MH):
                    for t in range(NT):
                        v.scalar_tensor_tensor(out=hs[:, t, h, :], in0=hs[:, t, h, :], scalar=hrs[:, NT * h + t:NT * h + t + 1],
                                               in1=og[:, t, h, :], op0=ALU.mult, op1=ALU.mult).then_inc(hn_ready, 1)

            def mla(r):
                v.wait_ge(prs_ready, 1)
                for t in range(NT):
                    v.tensor_scalar(pl[:, t, 0:QL], pl[:, t, 0:QL], acol[:, 12 + t:13 + t], None, ALU.mult).then_inc(pn_ready, 1)
                for t in range(NT):
                    v.scalar_tensor_tensor(out=pl[:, t, QL:QL + KVL], in0=pl[:, t, QL:QL + KVL], scalar=acol[:, 15 + t:16 + t],
                                           in1=g_kv[:, :], op0=ALU.mult, op1=ALU.mult).then_inc(pn_ready, 1)
                v.wait_ge(pl_ready, 12)
                for s in (0, 2, 3):
                    t = max(s - 1, 0)
                    for half in range(2):
                        ins = v.tensor_copy(kp2[:, s, half * ROPE:(half + 1) * ROPE], pl[:, t, QL + KVL:])
                ins.then_inc(kp_dup, 1)
                v.wait_ge(kp_full, 1)
                v.tensor_copy(kpT, ps[6][:, :]).then_inc(kp_ready, 1)
                v.wait_ge(kp_ready, 1)

                def rope(i, x):
                    v.wait_ge(rot_full, i + 1)
                    step(v.tensor_tensor(t_rot, ps[6][:, 0:LAT], trig[:, 1, :], ALU.mult))
                    step(v.tensor_tensor(t_cos, x, trig[:, 0, :], ALU.mult))
                    settle()
                    v.tensor_tensor(x, t_rot, t_cos, ALU.add).then_inc(rope_ready, 1)
                    v.wait_ge(rope_ready, i + 1)

                v.wait_ge(out_kv, 32)
                v.wait_ge(ck_full, 2)
                v.wait_ge(ql_full, 4)
                rope(0, kpT[:, KEYS - LAT:KEYS])
                for i in range(4):
                    v.wait_ge(qp_full, i + 1)
                    v.tensor_copy(qpT[:, i, :], ps[(3 * i + 2) % 4][:, 0:TOK]).then_inc(qp_raw, 1)
                v.wait_ge(qp_raw, 4)
                for i in range(4):
                    rope(i + 1, qpT[:, i, CTX:TOK])
                for c in range(8):
                    v.wait_ge(vt_full, c + 1)
                    i, s = c // 4, c % 4
                    v.tensor_copy(vt[:, s, 4 * i:4 * i + 4, :], ps[c % 4][:, :].rearrange("p (h n) -> p h n", h=4)).then_inc(vt_ready, 1)

                def peak(c):
                    n = CTX if c % NT == 0 else KEYS - CTX
                    v.wait_ge(sc_full, c + 1)
                    if c >= 4:
                        v.wait_ge(e_ready, c - 3)
                    step(v.tensor_reduce(acol[:, 28:29], ps[c % 3][:, 0:n], AX.X, ALU.max)); settle()
                    v.tensor_scalar(acol[:, 20 + c % 4:21 + c % 4], acol[:, 28:29], -SCALE, None, ALU.mult).then_inc(mx_ready, 1)
                    v.wait_ge(mx_ready, c + 1)

                peak(0)
                for c in range(NT * AH):
                    if c + 1 < NT * AH and (c + 1) % NT:
                        peak(c + 1)
                    n = CTX if c % NT == 0 else KEYS - CTX
                    v.wait_ge(e_ready, c + 1)
                    step(v.reciprocal(acol[:, 30 + c % 2:31 + c % 2], acol[:, 24 + c % 4:25 + c % 4])); settle()
                    v.tensor_scalar(pr[:, c % 2, 0:n], pr[:, c % 2, 0:n], acol[:, 30 + c % 2:31 + c % 2], None, ALU.mult)\
                     .then_inc(p_ready, 1)
                    if c % NT == NT - 1:
                        h = c // NT
                        if c + 1 < NT * AH:
                            peak(c + 1)
                        v.wait_ge(o_att, h + 1)
                        v.tensor_copy(hT[:, h, :], ps[5 + h % 2][:, 0:TOK]).then_inc(oT_ready, 1)

            def beaten_by(val, loss, cmp):
                for i in range(4):
                    step(v.memset(loss[:, :, i:i + 1], float(3 - i)))
                for d in range(1, 4):
                    step(v.tensor_tensor(cmp[d - 1][:, :, 0:4 - d], val[:, :, 0:4 - d], val[:, :, d:4], ALU.is_ge))
                settle()
                for d in range(1, 4):
                    c = cmp[d - 1][:, :, 0:4 - d]
                    step(v.tensor_tensor(loss[:, :, d:4], loss[:, :, d:4], c, ALU.add)); settle()
                    step(v.tensor_tensor(loss[:, :, 0:4 - d], loss[:, :, 0:4 - d], c, ALU.subtract)); settle()

            def experts(L, n):
                def tiles(a):
                    return a.rearrange("p (t e) -> p t e", t=NT)

                v.wait_ge(rt_e, L + 1)
                sc = rt[:, 1, :]
                step(v.tensor_scalar(sc, sc, 1.0, None, ALU.add)); settle()
                step(v.reciprocal(sc, sc)); settle()
                se = rt[:, 2, :]
                step(v.tensor_tensor(tiles(se), tiles(sc), b_rt[:, :].unsqueeze(1).to_broadcast([P, NT, NE]), ALU.add)); settle()
                loss = rt[:, 3, :]
                beaten_by(se.rearrange("p (g e) -> p g e", e=4), loss.rearrange("p (g e) -> p g e", e=4),
                          [rt[:, 13 + d, :].rearrange("p (g e) -> p g e", e=4) for d in range(3)])
                pick = rt[:, 5, :]
                step(v.tensor_scalar(pick, loss, 2.0, None, ALU.is_lt)); settle()
                top = rt[:, 6, :]
                step(v.tensor_tensor(top, pick, se, ALU.mult)); settle()
                gs = rt[:, 7, 0:12]
                step(v.tensor_reduce(gs, top.rearrange("p (g e) -> p g e", e=4), AX.X, ALU.add)); settle()
                gl = rt[:, 8, 0:12]
                beaten_by(gs.rearrange("p (t g) -> p t g", g=4), gl.rearrange("p (t g) -> p t g", g=4),
                          [rt[:, 13 + d, 0:12].rearrange("p (t g) -> p t g", g=4) for d in range(3)])
                gb = rt[:, 9, 0:12]
                step(v.tensor_scalar(gb, gl, 0.0, None, ALU.is_equal)); settle()
                by4 = lambda a: a.rearrange("p (g e) -> p g e", e=4)
                v.tensor_tensor(by4(pick), by4(pick), gb.unsqueeze(2).to_broadcast([P, 12, 4]), ALU.mult).then_inc(mask_ready, 1)
                v.wait_ge(mask_ready, L + 1)
                comb = rt[:, 0, :]
                step(v.tensor_tensor(comb, pick, sc, ALU.mult)); settle()
                sm = rt[:, 10, 0:3]
                step(v.tensor_reduce(sm, tiles(comb), AX.X, ALU.add)); settle()
                step(v.reciprocal(sm, sm)); settle()
                step(v.tensor_tensor(tiles(comb), tiles(comb), sm.unsqueeze(2).to_broadcast([P, NT, NE]), ALU.mult)); settle()
                v.wait_ge(pos_full, L + 1)
                pos = ps[6][:, 64:64 + 48]
                fits, sv, cv, more = rt[:, 16, :], rt[:, 17, :], rt[:, 18, :], rt[:, 11, :]
                step(v.scalar_tensor_tensor(out=fits, in0=pos, scalar=float(CAP), in1=pick, op0=ALU.is_lt, op1=ALU.mult))
                step(v.tensor_tensor(tiles(sv), tiles(pos), base[:, :].unsqueeze(1).to_broadcast([P, NT, NE]), ALU.add))
                settle()
                step(v.tensor_tensor(sv, sv, fits, ALU.mult))
                step(v.tensor_tensor(cv, comb, fits, ALU.mult))
                settle()
                hi = rt[:, 19, 0:3]
                step(v.tensor_reduce(hi, tiles(sv), AX.X, ALU.max)); settle()
                eq, lt = rt[:, 20, :], rt[:, 21, :]
                hib = hi.unsqueeze(2).to_broadcast([P, NT, NE])
                step(v.tensor_tensor(tiles(eq), tiles(sv), hib, ALU.is_equal))
                step(v.tensor_tensor(tiles(lt), tiles(sv), hib, ALU.is_lt))
                settle()
                step(v.tensor_tensor(lt, lt, sv, ALU.mult))
                step(v.tensor_tensor(eq, eq, cv, ALU.mult))
                settle()
                lo = rt[:, 19, 3:6]
                step(v.tensor_reduce(lo, tiles(lt), AX.X, ALU.max))
                step(v.tensor_reduce(rt[:, 12, 0:3], tiles(eq), AX.X, ALU.add))
                settle()
                both = rt[:, 19, 0:6]
                z = rt[:, 22, 0:6]
                step(v.tensor_scalar(z, both, 0.5, NOWHERE, ALU.is_lt, ALU.mult)); settle()
                step(v.tensor_tensor(z, z, both, ALU.add)); settle()
                step(v.tensor_scalar(slots[:, :], z, -1.0, None, ALU.add))
                step(v.tensor_reduce(rt[:, 22, 8:9], ps[6][:, 64 + 48:64 + 64], AX.X, ALU.max)); settle()
                v.tensor_scalar(spill[:, :], rt[:, 22, 8:9], float(CAP), None, ALU.is_gt).then_inc(slots_ready, 1)
                if L + 1 < LAYERS:
                    mod_columns(3 * (L + 1), 5)
                step(v.tensor_tensor(tiles(lt), tiles(sv), lo.unsqueeze(2).to_broadcast([P, NT, NE]), ALU.is_equal)); settle()
                step(v.tensor_tensor(lt, lt, cv, ALU.mult)); settle()
                step(v.tensor_reduce(rt[:, 12, 3:6], tiles(lt), AX.X, ALU.add))
                v.tensor_tensor(more, comb, cv, ALU.subtract).then_inc(f_comb, 1)
                settle()

                def tokens_of(G, par):
                    v.wait_ge(xt_full2, G * 2 + 2)
                    v.tensor_copy(xgT[:, par, 4:8, :].rearrange("p k s -> p (k s)"), ps[3][:, :]).then_inc(xb_ready, 1)

                def hidden(G, par):
                    v.wait_ge(sil_ready, G + 1)
                    v.wait_ge(gu_full, G * 2 + 2)
                    v.tensor_tensor(hid[:, par, :], sil[:, par, :], ps[par][:, FE:2 * FE], ALU.mult).then_inc(hid_ready, 1)

                def out(G, par, stored):
                    v.wait_ge(yp_full, G * 2 + 2)
                    v.wait_ge(y_stored[par], stored)
                    v.tensor_copy(ysb[:, par, 512:1024], ps[6][:, :]).then_inc(yb_ready, 1)

                def one(e, it):
                    G = NE * L + e if it is None else it * UNROLL + (NE * L + e)
                    hidden(G, e % 2)
                    if e + 1 < NE:
                        tokens_of(G + 1, (e + 1) % 2)
                    s0 = 16 * ((NE * L + e - 1) // 2 + 1)
                    out(G - 1, (e - 1) % 2, s0 if it is None else it * (8 * UNROLL) + s0)

                tokens_of(NE * L, 0)
                hidden(NE * L, 0)
                tokens_of(NE * L + 1, 1)
                with v.Fori(0, TURNS) as it:
                    for e in range(1, 1 + UNROLL):
                        one(e, it)
                for e in range(1 + TURNS * UNROLL, NE):
                    one(e, None)
                out(NE * L + NE - 1, 1, 16 * ((NE * L + NE - 1) // 2 + 1))
                for t in range(NT):
                    v.wait_ge(yg_in[t], 32 * (L + 1))
                    v.wait_ge(yw_ready, NT * L + t + 1)
                    v.scalar_tensor_tensor(out=yg[:, t, 0, :], in0=yg[:, t, 1, :], scalar=rt[:, 12, 3 + t:4 + t], in1=yg[:, t, 0, :],
                                           op0=ALU.mult, op1=ALU.add).then_inc(ys_ready, 1)
                gate = mod[:, L, 40:48, :]
                for t in range(NT):
                    a, b = t * P, (t + 1) * P
                    for c in range(KC):
                        v.wait_ge(yc_full, 2 * NT * L + 2 * t + c // 4 + 1)
                        ins = v.scalar_tensor_tensor(out=xT[:, c, a:b], in0=ps[2 * t + c // 4][:, (c % 4) * P:(c % 4 + 1) * P],
                                                     scalar=gate[:, c, min(t, 1):min(t, 1) + 1], in1=xT[:, c, a:b],
                                                     op0=ALU.mult, op1=ALU.add)
                        if t == NT - 1:
                            ins.then_inc(x_ready, 1)
                if L + 1 < LAYERS:
                    mod_columns(3 * (L + 1) + 1, 6)
                over = v.value_load(spill[0:1, 0:1], min_val=0, max_val=1)
                with v.If(over > 0):
                    v.wait_ge(x_ready, 8 * (n + 2))
                    v.wait_ge(f_combT, L + 1)
                    v.tensor_copy(combT[0:NE, :], ps[4][0:NE, 0:TOK]).then_inc(f_combT_ready, 1)
                    v.memset(yacc[:, :, :], 0.0).then_inc(f_zero, 1)
                    v.wait_ge(f_zero, L + 1)
                    with v.Fori(0, NE) as it:
                        G = it + NE * L
                        for f in range(2):
                            v.wait_ge(f_sg, G * 2 + (f + 1))
                            v.wait_ge(f_gu, G * 4 + (3 + f))
                            v.wait_ge(f_cb, G + 1)
                            v.tensor_tensor(sg[:, f, :], sg[:, f, :], ps[2 + f][:, 0:TOK], ALU.mult).then_inc(f_step, 1)
                            v.wait_ge(f_step, G * 2 + (f + 1))
                            v.tensor_tensor(hidF[:, f, :], sg[:, f, :], ps[4][:, 0:TOK], ALU.mult).then_inc(f_hid, 1)
                        for c in range(KC):
                            v.wait_ge(f_y, G * 8 + (c + 1))
                            v.tensor_tensor(yacc[:, c, :], yacc[:, c, :], ps[5 + c % 2][:, 0:TOK], ALU.add).then_inc(f_yused, 1)
                    v.wait_ge(f_yused, 8 * NE * (L + 1))
                    for c in range(KC):
                        for q in range(2):
                            a, b = SPAN[q]
                            ins = v.scalar_tensor_tensor(out=xT[:, c, a:b], in0=yacc[:, c, a:b], scalar=gate[:, c, q:q + 1],
                                                         in1=xT[:, c, a:b], op0=ALU.mult, op1=ALU.add)
                    ins.then_inc(spill_done, 1)
                with v.Else():
                    v.sem_inc(f_combT_ready, 1)
                    v.sem_inc(f_zero, 1)
                    v.sem_inc(f_step, 2 * NE)
                    v.sem_inc(f_hid, 2 * NE)
                    v.sem_inc(f_yused, 8 * NE)
                    v.sem_inc(spill_done, 1)

            mod_columns(0, 5)
            for L in range(LAYERS):
                kind = L % 3
                norm(2 * L, amp[:, 0, :, :])
                if kind == 0:
                    pool_mixer(2 * L)
                elif kind == 1:
                    mlstm(2 * L)
                else:
                    mla(2 * L)
                residual(2 * L, gpool if kind == 0 else mod[:, L, 16:24, :], lambda c: ps[c % 4], 8 * L)
                mod_columns(3 * L + 2, 7)
                norm(2 * L + 1, amp[:, 1, :, :])
                experts(L, 2 * L + 1)
            norm(2 * LAYERS, vecs[:, 80:88])

        @block.gpsimd
        def _(g):
            g.memset(ones[:, :], 1.0).then_inc(pool_set, 1)
            g.memset(mean_ones[:, :], 1.0 / D).then_inc(pool_set, 1)
            g.memset(eps[:, :], EPS).then_inc(pool_set, 1)

            def pooling_tables(n):
                for a, b in ((0, PAD), (PAD + CTX, 2 * PAD + CTX), (HP - PAD, HP)):
                    g.memset(hp[:, :, a:b], 0.0).then_inc(pads_set, 1)
                g.dma_start(inv[:, :, :], A["k_inv"].partition_broadcast(P)).then_inc(inv_in, 16)

            g.wait_ge(vec_t, 1)
            g.wait_ge(xt_full, KC)
            pooling_tables(0)
            g.memset(zeros, 0.0).then_inc(zeros_set, 1)
            g.wait_ge(zeros_set, 1)
            g.wait_ge(ada_unit, 8)
            for e in range(NE):
                g.dma_start(Xg[e * SLOTS:(e + 1) * SLOTS, :], zeros).then_inc(zeroed if e > 1 else y_stored[e], 16)
            g.wait_ge(zeroed, 16 * (NE - 2))
            for i in range(2):
                g.wait_ge(y_stored[i], 16)

            def at_slot(j):
                return bass.IndirectOffsetOnAxis(ap=slots[:, j:j + 1], axis=0)

            def experts(L):
                g.wait_ge(slots_ready, L + 1)
                for t in range(NT):
                    g.wait_ge(ht_ready, 2 * NT * L + 2 * t + 2)
                    for q in range(2):
                        g.indirect_dma_start(out=Xg, out_offset=at_slot(q * NT + t), in_=htok[:, t, :], in_offset=None,
                                             bounds_check=NE * SLOTS - 1, oob_is_err=False).then_inc(scattered, 16)
                g.wait_ge(scattered, 16 * 2 * NT * (L + 1))
                for par in range(2):
                    g.dma_start(xg[:, par, :], Xg[par * SLOTS:(par + 1) * SLOTS, :]).then_inc(xg_in[par], 16)

                def store(G, rows, par):
                    g.wait_ge(ya_ready, G + 1)
                    g.wait_ge(yb_ready, G + 2)
                    g.wait_ge(slots_ready, L + 1)
                    g.dma_start(Yg[rows, :], ysb[:, par, :]).then_inc(y_stored[par], 16)

                def fetch(G, rows, par):
                    g.wait_ge(xt_full2, G * 2 + 2)
                    g.sem_inc(f_free, 1)
                    g.dma_start(xg[:, par, :], Xg[rows, :]).then_inc(xg_in[par], 16)

                fetch(NE * L, slice(2 * SLOTS, 3 * SLOTS), 0)
                with g.Fori(0, NE // 2 - 2) as it:
                    for par in range(2):
                        G = it * 2 + (NE * L + par)
                        fetch(G + 1, bass.ds(it * (2 * SLOTS) + (3 + par) * SLOTS, SLOTS), 1 - par)
                        store(G, bass.ds(it * (2 * SLOTS) + par * SLOTS, SLOTS), par)
                for e in range(NE - 4, NE):
                    if e + 3 < NE:
                        fetch(NE * L + e + 1, slice((e + 3) * SLOTS, (e + 4) * SLOTS), (e + 1) % 2)
                    store(NE * L + e, slice(e * SLOTS, (e + 1) * SLOTS), e % 2)
                for par in range(2):
                    g.wait_ge(y_stored[par], 16 * (NE // 2 * (L + 1) + 1))
                for t in range(NT):
                    for q in range(2):
                        g.indirect_dma_start(out=yg[:, t, q, :], out_offset=None, in_=Yg, in_offset=at_slot(q * NT + t),
                                             bounds_check=NE * SLOTS - 1, oob_is_err=False).then_inc(yg_in[t], 16)
                over = g.value_load(spill[0:1, 0:1], min_val=0, max_val=1)
                with g.If(over > 0):
                    g.wait_ge(f_combT_ready, L + 1)
                    g.dma_start(comb_row[0:1, :, :], combT[0:NE, :]).then_inc(f_rows, 16)
                    g.wait_ge(f_rows, 16 * (L + 1))
                    with g.Fori(0, NE) as it:
                        for n, (name, k) in enumerate((("w_exp_gate", KC), ("w_exp_up", KC), ("w_exp_down", 2))):
                            if n:
                                g.wait_ge(f_gu, it * 4 + (4 * NE * L + 2 * n))
                                g.sem_inc(f_free, 1)
                            g.dma_start(wF.rearrange("p (k n) -> p k n", k=k),
                                        A[name][L, bass.ds(it, 1)].rearrange("e (k p) n -> p (e k) n", p=P)).then_inc(f_w, 16)
                            g.wait_ge(f_w, it * 48 + (48 * NE * L + 16 * (n + 1)))
                        g.wait_ge(f_y, it * 8 + (8 * NE * L + 8))
                with g.Else():
                    g.sem_inc(f_rows, 16)
                    g.sem_inc(f_w, 48 * NE)

            experts(0)
            g.wait_ge(x_ready, 24)
            g.wait_ge(spill_done, 1)
            g.memset(vx[:, :, :, DV:VX], 1.0).then_inc(vx_ones, 1)
            g.dma_start(mask[:, :, :], A["k_mask"]).then_inc(tables_in, 16)
            g.dma_start(sel, A["k_sel"]).then_inc(tables_in, 16)
            for d in range(2):
                g.dma_start(cx[:, d, :, 0:DV], A["state_mlstm_C"][0, 0, d].rearrange("h k v -> k h v")).then_inc(state_in, 16)
            with nc.allow_non_contiguous_dma(reason="eight floats"):
                g.wait_ge(rows_done, 1)
                g.dma_start(O["new_m"][0, 0, 0].rearrange("(h o) -> h o", o=1), rE[:, 0, CTX - 1:CTX]).then_inc(out_m, 16)
                g.dma_start(O["new_m"][0, 0, 1].rearrange("(h o) -> h o", o=1), rE[:, 1, 0:1]).then_inc(out_m, 16)
            for h in range(MH):
                for d in range(2):
                    g.wait_ge(c_copied, 2 * h + d + 1)
                    g.dma_start(O["new_C"][0, 0, d, h], c_st).then_inc(out_c, 16)
            g.wait_ge(n_copied, 1)
            g.dma_start(O["new_n"].rearrange("b l d h k -> (b l d h) k"), n_t[0:8, :]).then_inc(out_n, 16)
            g.wait_ge(out_m, 32)
            g.wait_ge(out_c, 16 * 8)
            g.wait_ge(out_n, 16)
            experts(1)
            g.wait_ge(pl_full, 12)
            g.dma_start(cache, A["cache_mla_ckv"][0, 0]).then_inc(cache_in, 16)
            for half in range(2):
                g.dma_start(kp2[:, 1, half * ROPE:(half + 1) * ROPE], A["cache_mla_kpe"][0, 0]).then_inc(cache_in, 16)
            g.wait_ge(pl_ready, 12)
            g.dma_start(O["new_kpe"][0, 0], pl[:, 0, QL + KVL:]).then_inc(out_kv, 16)
            g.wait_ge(pn_ready, 4)
            g.dma_start(O["new_ckv"][0, 0], pl[:, 0, QL:QL + KVL]).then_inc(out_kv, 16)
            g.wait_ge(out_kv, 32)
            experts(2)
            g.wait_ge(x_ready, 56)
            g.wait_ge(spill_done, 3)
            pooling_tables(1)
            g.wait_ge(inv_in, 32)
            experts(3)


INPUTS = ["x_prompt", "x_sample", "state_mlstm_C", "state_mlstm_n", "state_mlstm_m", "cache_mla_ckv", "cache_mla_kpe",
          "c", "c_ctx", "w_ada", "b_ada", "norm_mix", "norm_ffn", "norm_final", "w_pool", "pool_scale", "w_mlstm_in",
          "b_mlstm_gate", "mlstm_head_g", "w_mlstm_out", "w_mla_in", "mla_q_g", "mla_kv_g", "w_mla_qb", "w_mla_kvb",
          "w_mla_out", "w_router", "b_router", "w_exp_gate", "w_exp_up", "w_exp_down"]
OUTPUTS = [("y_prompt", (1, CTX, D)), ("y_sample", (1, LAT, D)), ("new_C", (1, 1, 2, MH, DK, DV)),
           ("new_n", (1, 1, 2, MH, DK)), ("new_m", (1, 1, 2, MH)), ("new_ckv", (1, 1, CTX, KVL)),
           ("new_kpe", (1, 1, CTX, ROPE))]


def kernel(**inputs):
    import concourse.bacc as bacc
    from concourse.bass_utils import run_bass_kernel_spmd

    nc = bacc.Bacc("TRN2", target_bir_lowering=False, num_devices=1)
    arrays = {name: np.ascontiguousarray(inputs[name]) for name in INPUTS}
    arrays.update(constants())
    A = {name: nc.dram_tensor("in_" + name, a.shape, mybir.dt.from_np(a.dtype), kind="ExternalInput").ap()
         for name, a in arrays.items()}
    O = {name: nc.dram_tensor("out_" + name, shape, F32, kind="ExternalOutput").ap() for name, shape in OUTPUTS}
    Xg = nc.dram_tensor("slot_in", (NE * SLOTS, D), F32).ap()
    Yg = nc.dram_tensor("slot_out", (NE * SLOTS, D), F32).ap()
    build(nc, A, O, Xg, Yg)
    r = run_bass_kernel_spmd(nc, [{"in_" + k: a for k, a in arrays.items()}], core_ids=[0])
    return tuple(r.results[0]["out_" + name] for name, _ in OUTPUTS)
```
